# Optimizing a Trainium2 kernel written in Bass

```python
import jax, jax.numpy as jnp
from jax import lax
import numpy as np

D_MODEL = 1024
BATCH = 1
SEQ = 1024
DEPTH = 1

HEAD = 64
RMS_EPS = 1e-6
A_WIDTH = D_MODEL
A_HEADS = A_WIDTH // HEAD
DECAY_LORA = 64
ICL_LORA = 64
GATE_LORA = 128
VRES_LORA = 32
A_COLS = 3 * A_WIDTH + DECAY_LORA + ICL_LORA + GATE_LORA
A_SPLITS = (A_WIDTH, 2 * A_WIDTH, 3 * A_WIDTH, 3 * A_WIDTH + DECAY_LORA, 3 * A_WIDTH + DECAY_LORA + ICL_LORA)
GN_EPS = 64e-5
DILATION_GROUPS = ((128, 1), (512, 4), (2048, 16))
B_HEADS_PER_GROUP = 4
B_HEADS = B_HEADS_PER_GROUP * len(DILATION_GROUPS)
B_WIDTH = B_HEADS * HEAD
B_OUT = B_HEADS_PER_GROUP * HEAD
B_COLS = 3 * B_WIDTH
DIL_BLOCK = 128
ROPE_THETA = 10000.0
C_WIDTH = D_MODEL
C_GROUPS = 8
C_CHUNK = 128
C_COLS = 2 * C_WIDTH
LN_EPS = 1e-5
N_BRANCHES = 3
GATE_COLS = N_BRANCHES * D_MODEL
IN_COLS = A_COLS + B_COLS + C_COLS + GATE_COLS
IN_SPLITS = (A_COLS, A_COLS + B_COLS, A_COLS + B_COLS + C_COLS)
N_GROUPS = 4
EXPERTS_PER_GROUP = 8
N_EXPERTS = N_GROUPS * EXPERTS_PER_GROUP
TOP_K = 2
EXPERT_FF = D_MODEL // 2
MOE_BLOCK = 256

kernel_name = "hybrid_rwkv7_dilated_gmlp_hiermoe"

f32 = jnp.float32

def rms_norm(x, g):
    xf = x.astype(f32)
    y = xf * lax.rsqrt(jnp.mean(xf * xf, axis=-1, keepdims=True) + RMS_EPS)
    return y.astype(x.dtype) * g

def token_shift_lerp(z, mu):
    prev = jnp.pad(z, ((0, 0), (1, 0), (0, 0)))[:, :-1]
    return z + (prev - z) * mu

def wkv7_scan(r, decay, k, v, a, b):
    Bsz, T, H, N = r.shape

    def step(S, inp):
        r_t, w_t, k_t, v_t, a_t, b_t = inp
        Sa = jnp.einsum('bhij,bhj->bhi', S, a_t)
        S = S * w_t[:, :, None, :] + Sa[..., None] * b_t[:, :, None, :] + v_t[..., None] * k_t[:, :, None, :]
        return S, jnp.einsum('bhij,bhj->bhi', S, r_t)

    seq = tuple(jnp.moveaxis(z.astype(f32), 1, 0) for z in (r, decay, k, v, a, b))
    _, y = lax.scan(step, jnp.zeros((Bsz, H, N, N), f32), seq)
    return jnp.moveaxis(y, 0, 1)

def rwkv7_time_mix(r, k, v, w_lo, a_lo, g_lo, w0, w2, a0, a2, g2, k_k, k_a, r_k, lnx_w, lnx_b):
    Bsz, T, _ = r.shape
    heads = lambda z: z.reshape(Bsz, T, A_HEADS, HEAD)
    w = -jax.nn.softplus(-(w0 + jnp.tanh(w_lo) @ w2).astype(f32)) - 0.5
    decay = jnp.exp(-jnp.exp(w))
    a = jax.nn.sigmoid((a0 + a_lo @ a2).astype(f32))
    g = jax.nn.sigmoid(g_lo) @ g2
    kk = heads((k * k_k).astype(f32))
    kk = kk / jnp.maximum(jnp.sqrt(jnp.sum(kk * kk, axis=-1, keepdims=True)), 1e-12)
    k = k.astype(f32) * (1.0 + (a - 1.0) * k_a.astype(f32))
    rh, kh, vh, ah = heads(r.astype(f32)), heads(k), heads(v.astype(f32)), heads(a)
    y = wkv7_scan(rh, heads(decay), kh, vh, -kk, kk * ah)
    mean = jnp.mean(y, axis=-1, keepdims=True)
    var = jnp.mean(jnp.square(y - mean), axis=-1, keepdims=True)
    y = (y - mean) * lax.rsqrt(var + GN_EPS)
    y = y.reshape(Bsz, T, A_WIDTH) * lnx_w.astype(f32) + lnx_b.astype(f32)
    bonus = jnp.sum(rh * kh * r_k.astype(f32), axis=-1, keepdims=True) * vh
    y = y + bonus.reshape(Bsz, T, A_WIDTH)
    return (y * g.astype(f32)).astype(r.dtype)

def rotary(z, cos, sin):
    z1, z2 = jnp.split(z.astype(f32), 2, axis=-1)
    c, s = cos[:, None, :], sin[:, None, :]
    return jnp.concatenate([z1 * c - z2 * s, z1 * s + z2 * c], axis=-1).astype(z.dtype)

def dilated_group_attention(q, k, v, dilation, span):
    Bsz, T, Hg, hd = q.shape
    L = T // dilation
    nb = -(-L // DIL_BLOCK)
    Lp = nb * DIL_BLOCK

    def strided(z):
        z = z.reshape(Bsz, L, dilation, Hg, hd).transpose(0, 2, 3, 1, 4)
        return jnp.pad(z, ((0, 0), (0, 0), (0, 0), (0, Lp - L), (0, 0)))

    def windows(z):
        z = jnp.pad(strided(z), ((0, 0), (0, 0), (0, 0), (DIL_BLOCK, 0), (0, 0)))
        z = z.reshape(Bsz, dilation, Hg, nb + 1, DIL_BLOCK, hd)
        return jnp.concatenate([z[:, :, :, :-1], z[:, :, :, 1:]], axis=-2)

    qs = strided(q).reshape(Bsz, dilation, Hg, nb, DIL_BLOCK, hd).astype(f32)
    ks, vs = windows(k).astype(f32), windows(v).astype(f32)
    s = jnp.einsum('bdhnqc,bdhnkc->bdhnqk', qs, ks) * (hd ** -0.5)
    qi = jnp.arange(DIL_BLOCK)[:, None]
    kj = jnp.arange(2 * DIL_BLOCK)[None, :]
    dist = qi + DIL_BLOCK - kj
    key_idx = jnp.arange(nb)[:, None, None] * DIL_BLOCK - DIL_BLOCK + kj
    mask = (dist >= 0) & (dist <= span) & (key_idx >= 0)
    s = jnp.where(mask, s, -jnp.inf)
    m = jnp.max(s, axis=-1, keepdims=True)
    e = jnp.exp(s - m)
    den = jnp.sum(e, axis=-1, keepdims=True)
    o = jnp.einsum('bdhnqk,bdhnkc->bdhnqc', e, vs) / den
    lse = (m + jnp.log(den))[..., 0]

    def unstride(z):
        z = z.reshape(Bsz, dilation, Hg, Lp, *z.shape[5:])[:, :, :, :L]
        z = jnp.moveaxis(z, 3, 1)
        return z.reshape(Bsz, T, Hg, *z.shape[4:])

    return unstride(o), unstride(lse)

def dilated_attention(q, k, v):
    outs, lses = [], []
    for gi, (window, dilation) in enumerate(DILATION_GROUPS):
        sl = slice(gi * B_HEADS_PER_GROUP, (gi + 1) * B_HEADS_PER_GROUP)
        o, lse = dilated_group_attention(q[:, :, sl], k[:, :, sl], v[:, :, sl], dilation, window // dilation)
        outs.append(o)
        lses.append(lse)
    wts = jax.nn.softmax(jnp.stack(lses, axis=0), axis=0)
    o = jnp.einsum('gbth,gbthc->bthc', wts, jnp.stack(outs, axis=0))
    Bsz, T = q.shape[:2]
    return o.reshape(Bsz, T, B_OUT).astype(q.dtype)

def spatial_gating(zc, ln_w, ln_b, ws, bs):
    z = jax.nn.gelu(zc, approximate=False)
    u, v = jnp.split(z, 2, axis=-1)
    vf = v.astype(f32)
    mean = jnp.mean(vf, axis=-1, keepdims=True)
    var = jnp.mean(jnp.square(vf - mean), axis=-1, keepdims=True)
    v = ((vf - mean) * lax.rsqrt(var + LN_EPS)).astype(v.dtype) * ln_w + ln_b
    Bsz, T, _ = v.shape
    vg = v.reshape(Bsz, T // C_CHUNK, C_CHUNK, C_GROUPS, C_WIDTH // C_GROUPS)
    ws_causal = ws * jnp.tril(jnp.ones((C_CHUNK, C_CHUNK), ws.dtype))
    mixed = jnp.einsum('gts,bnsgc->bntgc', ws_causal, vg) + bs.T[:, :, None]
    return u * mixed.reshape(Bsz, T, C_WIDTH)

def hierarchical_moe(h, rg, rgb, re, reb, w1, w3, w2):
    Bsz, T, D = h.shape
    N = Bsz * T
    NK = N * TOP_K
    xf = h.reshape(N, D)
    glog = (xf @ rg + rgb).astype(f32)
    gprob = jax.nn.softmax(glog, axis=-1)
    gsel = jnp.argmax(glog, axis=-1)
    p_g = jnp.take_along_axis(gprob, gsel[:, None], axis=1)[:, 0]
    elog = (xf @ re + reb).astype(f32).reshape(N, N_GROUPS, EXPERTS_PER_GROUP)
    elog_g = jnp.take_along_axis(elog, gsel[:, None, None], axis=1)[:, 0]
    top_v, top_i = lax.top_k(elog_g, TOP_K)
    wts = jax.nn.softmax(top_v, axis=-1) * p_g[:, None]
    eid = gsel[:, None] * EXPERTS_PER_GROUP + top_i
    flat_e = eid.reshape(-1).astype(jnp.int32)
    flat_t = jnp.repeat(jnp.arange(N, dtype=jnp.int32), TOP_K)
    flat_w = wts.reshape(-1)
    order = jnp.argsort(flat_e)
    se, st, sw = flat_e[order], flat_t[order], flat_w[order]
    counts = jnp.bincount(flat_e, length=N_EXPERTS)
    padded = (counts + MOE_BLOCK - 1) // MOE_BLOCK * MOE_BLOCK
    pend = jnp.cumsum(padded)
    pstart = pend - padded
    cstart = jnp.cumsum(counts) - counts
    dest = pstart[se] + jnp.arange(NK, dtype=jnp.int32) - cstart[se]
    nblk = -(-NK // MOE_BLOCK) + N_EXPERTS
    P = nblk * MOE_BLOCK
    tok_buf = jnp.full((P,), N, jnp.int32).at[dest].set(st)
    w_buf = jnp.zeros((P,), f32).at[dest].set(sw)
    blk_e = jnp.minimum(jnp.searchsorted(pend, jnp.arange(nblk) * MOE_BLOCK, side='right'), N_EXPERTS - 1)
    xpad = jnp.concatenate([xf, jnp.zeros((1, D), xf.dtype)], axis=0)
    xb = xpad[tok_buf].reshape(nblk, MOE_BLOCK, D)

    def expert_block(args):
        xblk, e = args
        hid = jax.nn.silu(xblk @ w1[e]) * (xblk @ w3[e])
        return hid @ w2[e]

    yb = lax.map(expert_block, (xb, blk_e)).reshape(P, D)
    y = jax.ops.segment_sum(yb * w_buf[:, None].astype(yb.dtype), tok_buf, num_segments=N + 1)[:N]
    return y.reshape(Bsz, T, D)

def setup_inputs(seed: int = 0) -> dict:
    key = jax.random.key(seed)
    ks = iter(jax.random.split(key, 48))
    nrm = lambda shape, scale: scale * jax.random.normal(next(ks), shape, f32)
    unif = lambda shape, lo, hi: jax.random.uniform(next(ks), shape, f32, lo, hi)
    L, D = DEPTH, D_MODEL
    return {
        "x": nrm((BATCH, SEQ, D), 1.0),
        "norm_mix": 1.0 + nrm((L, D), 0.02),
        "w_in": nrm((L, D, IN_COLS), D ** -0.5),
        "mu_a": unif((L, A_COLS), 0.0, 1.0),
        "w_decay0": unif((L, A_WIDTH), -6.0, -1.0),
        "w_decay2": nrm((L, DECAY_LORA, A_WIDTH), 0.1),
        "a0": nrm((L, A_WIDTH), 0.1),
        "a2": nrm((L, ICL_LORA, A_WIDTH), 0.5 * ICL_LORA ** -0.5),
        "g2": nrm((L, GATE_LORA, A_WIDTH), GATE_LORA ** -0.5),
        "k_k": 0.85 + nrm((L, A_WIDTH), 0.02),
        "k_a": 1.0 + nrm((L, A_WIDTH), 0.02),
        "r_k": nrm((L, A_HEADS, HEAD), 0.1),
        "lnx_w": 1.0 + nrm((L, A_WIDTH), 0.02),
        "lnx_b": nrm((L, A_WIDTH), 0.02),
        "vres_mu": unif((L - 1, VRES_LORA), 0.0, 1.0),
        "vres_w1": nrm((L - 1, D, VRES_LORA), D ** -0.5),
        "vres_w2": nrm((L - 1, VRES_LORA, A_WIDTH), 0.5 * VRES_LORA ** -0.5),
        "vres_b": 1.0 + nrm((L - 1, A_WIDTH), 0.1),
        "sgu_ln_w": 1.0 + nrm((L, C_WIDTH), 0.02),
        "sgu_ln_b": nrm((L, C_WIDTH), 0.02),
        "sgu_ws": nrm((L, C_GROUPS, C_CHUNK, C_CHUNK), C_CHUNK ** -0.5),
        "sgu_bs": 1.0 + nrm((L, C_GROUPS, C_CHUNK), 0.02),
        "gate_b": nrm((L, N_BRANCHES, D), 0.1),
        "w_pa": nrm((L, A_WIDTH, D), A_WIDTH ** -0.5),
        "w_pb": nrm((L, B_OUT, D), B_OUT ** -0.5),
        "w_pc": nrm((L, C_WIDTH, D), C_WIDTH ** -0.5),
        "w_out": nrm((L, D, D), D ** -0.5),
        "norm_ffn": 1.0 + nrm((L, D), 0.02),
        "router_grp": nrm((L, D, N_GROUPS), D ** -0.5),
        "router_grp_b": nrm((L, N_GROUPS), 0.01),
        "router_exp": nrm((L, D, N_EXPERTS), D ** -0.5),
        "router_exp_b": nrm((L, N_EXPERTS), 0.01),
        "moe_w1": nrm((L, N_EXPERTS, D, EXPERT_FF), D ** -0.5),
        "moe_w3": nrm((L, N_EXPERTS, D, EXPERT_FF), D ** -0.5),
        "moe_w2": nrm((L, N_EXPERTS, EXPERT_FF, D), EXPERT_FF ** -0.5),
        "norm_final": 1.0 + nrm((D,), 0.02),
    }

def reference(x, norm_mix, w_in, mu_a, w_decay0, w_decay2, a0, a2, g2, k_k, k_a, r_k, lnx_w, lnx_b,
              vres_mu, vres_w1, vres_w2, vres_b, sgu_ln_w, sgu_ln_b, sgu_ws, sgu_bs, gate_b,
              w_pa, w_pb, w_pc, w_out, norm_ffn, router_grp, router_grp_b, router_exp, router_exp_b,
              moe_w1, moe_w3, moe_w2, norm_final):
    Bsz, T, D = x.shape
    pos = jnp.arange(T, dtype=f32)
    inv_freq = ROPE_THETA ** (-jnp.arange(0, HEAD, 2, dtype=f32) / HEAD)
    ang = pos[:, None] * inv_freq[None, :]
    cos, sin = jnp.cos(ang), jnp.sin(ang)
    v_first = None
    for l in range(DEPTH):
        h = rms_norm(x, norm_mix[l])
        proj = h @ w_in[l]
        za, zb, zc, zg = jnp.split(proj, IN_SPLITS, axis=-1)
        za = token_shift_lerp(za, mu_a[l])
        r, k, v, w_lo, a_lo, g_lo = jnp.split(za, A_SPLITS, axis=-1)
        if l == 0:
            v_first = v
        else:
            vlo = token_shift_lerp(h @ vres_w1[l - 1], vres_mu[l - 1])
            v = v + (v_first - v) * jax.nn.sigmoid(vres_b[l - 1] + vlo @ vres_w2[l - 1])
        ya = rwkv7_time_mix(r, k, v, w_lo, a_lo, g_lo, w_decay0[l], w_decay2[l], a0[l], a2[l], g2[l],
                            k_k[l], k_a[l], r_k[l], lnx_w[l], lnx_b[l])
        qb, kb, vb = (z.reshape(Bsz, T, B_HEADS, HEAD) for z in jnp.split(zb, 3, axis=-1))
        yb = dilated_attention(rotary(qb, cos, sin), rotary(kb, cos, sin), vb)
        yc = spatial_gating(zc, sgu_ln_w[l], sgu_ln_b[l], sgu_ws[l], sgu_bs[l])
        gates = jax.nn.sigmoid(zg.reshape(Bsz, T, N_BRANCHES, D) + gate_b[l])
        merged = (gates[:, :, 0] * (ya @ w_pa[l]) + gates[:, :, 1] * (yb @ w_pb[l])
                  + gates[:, :, 2] * (yc @ w_pc[l]))
        x = x + merged @ w_out[l]
        x = x + hierarchical_moe(rms_norm(x, norm_ffn[l]), router_grp[l], router_grp_b[l], router_exp[l],
                                 router_exp_b[l], moe_w1[l], moe_w3[l], moe_w2[l])
    return rms_norm(x, norm_final)


_drawn_inputs = setup_inputs


def setup_inputs(seed=0):
    import zlib

    import numpy as np

    out = dict(_drawn_inputs(seed))
    spreads = {}
    factors = {'k_k': 18.621,
     'k_a': 3.945,
     'lnx_w': 16.15,
     'lnx_b': 16.056,
     'sgu_ln_w': 19.741,
     'sgu_ln_b': 20.273,
     'sgu_bs': 15.235,
     'router_grp_b': 12.319,
     'router_exp_b': 16.467,
     'norm_final': 8.66,
     'norm_ffn': 4.352}
    for name, (base, spread) in spreads.items():
        noise = np.random.default_rng([zlib.crc32(name.encode()), seed]).standard_normal(out[name].shape)
        drawn = base * np.exp(spread * noise) if base else spread * noise
        out[name] = __import__('jax').numpy.asarray(drawn.astype(out[name].dtype))
    for name, factor in factors.items():
        out[name] = (out[name] * factor).astype(out[name].dtype)
    return out
```

```python
from contextlib import ExitStack

import concourse.bass as bass
from concourse import mybir
import numpy as np

F32 = mybir.dt.float32
I32 = mybir.dt.int32
U32 = mybir.dt.uint32
ALU = mybir.AluOpType
ACT = mybir.ActivationFunctionType
AX = mybir.AxisListType
ds = bass.ds

P = 128
T = 1024
D = 1024
KT = D // P
NT = T // P
HALF = 512
HEAD = 64
A_WIDTH = D
PAIRS = A_WIDTH // P
CH = 64
NCH = T // CH
QC = 4
NQ = NCH // QC
A_COLS = 3 * A_WIDTH + 256
B_GROUP_HEADS = 4
B_OUT = B_GROUP_HEADS * HEAD
B_WIDTH = 3 * B_OUT
B_COLS = 3 * B_WIDTH
C_WIDTH = D
IN_COLS = A_COLS + B_COLS + 2 * C_WIDTH + 3 * D
COL_B = A_COLS
COL_C = A_COLS + B_COLS
COL_G = COL_C + 2 * C_WIDTH
RMS_EPS = 1e-6
GN_EPS = 64e-5
LN_EPS = 1e-5
DECAY_SCALE = float(np.exp(-0.5))
N_GROUPS = 4
PER_GROUP = 8
N_EXPERTS = N_GROUPS * PER_GROUP
FF = D // 2
SLOTS = P
MAX_EXTRA = 2 * T // SLOTS - 1
NEG = -1e30

ROWS = {}
_n = 0
for _name, _tiles in (("norm_mix", 8), ("gate_b", 24), ("w_decay0", 8), ("a0", 8), ("k_k", 8), ("k_a", 8),
                      ("r_k", 8), ("lnx_w", 8), ("lnx_b", 8), ("mu_a", 26), ("norm_ffn", 8)):
    ROWS[_name] = (_n, _tiles)
    _n += _tiles
N_ROWS = _n
W0, A0, K_K, K_A, R_K, LNX_W, LNX_B, MU_R, MU_K, MU_V = range(10)
N_PAIR = 10


def level_masks():
    t, s = np.meshgrid(np.arange(P), np.arange(P), indexing="ij")
    masks = []
    m = 1
    while m < CH:
        masks.append((t // (2 * m) == s // (2 * m)) & (t // m % 2 == 1) & (s // m % 2 == 0))
        m *= 2
    return np.stack(masks).astype(np.float32)


LEVELS = 6


def constants():
    c = {}
    p = np.arange(P)
    row, col = np.meshgrid(p, p, indexing="ij")
    same = row // CH == col // CH
    c["ident"] = np.eye(P)
    c["ones"] = np.ones((P, P))
    c["ones_bd"] = same
    strict = same & (row < col)
    upto = same & (row <= col)
    c["gram_mask"] = np.concatenate([upto, strict], 1)
    lm = level_masks()
    c["level_mask"] = lm.transpose(1, 0, 2).reshape(P, -1)
    c["level1_up"] = lm[0].T
    c["running"] = np.tile((np.arange(T) % CH != 0)[None], (P, 1))
    inv = (np.float32(10000.0) ** (-np.arange(0, HEAD, 2, dtype=np.float32) / np.float32(HEAD))).astype(np.float32)
    ang = (np.arange(T, dtype=np.float32)[None] * inv[:, None]).astype(np.float32)
    cos, sin = np.cos(ang), np.sin(ang)
    c["rope_cos"] = np.concatenate([cos] * 4)
    c["rope_sin"] = np.concatenate([-sin, sin, -sin, sin])
    swap = np.zeros((P, P))
    swap[(p // 64) * 64 + (p + 32) % 64, p] = 1
    c["swap"] = swap
    prev = np.where(col >= row, 0, NEG)
    own = np.where(col <= row, 0, NEG)
    c["mask_two"] = np.concatenate([prev, own], 1)
    c["mask_pair"] = np.where((col <= row) & (row % 2 == col % 2), 0, NEG)
    c["before"] = row < col
    c["thresholds"] = np.tile((np.arange(1, 8) * SLOTS)[None], (P, 1))
    c["expert_ids"] = np.tile(np.arange(N_EXPERTS)[None], (P, 1))
    c["extra_ids"] = np.tile(np.arange(MAX_EXTRA)[None], (P, 1))
    c["token_ids"] = p[:, None] + P * np.arange(NT)[None]
    c["causal"] = row <= col
    return {k: np.ascontiguousarray(v, dtype=np.float32) for k, v in c.items()}


class Steps:

    def __init__(self, sem, names, lead):
        self.sem, self.names, self.lead, self.seen = sem, names, lead, 0

    def start(self, engine):
        engine.sem_inc(self.sem, self.lead * len(self.names))

    def mark(self, name):
        assert self.names[self.seen % len(self.names)] == name, (name, self.names[self.seen % len(self.names)])
        self.seen += 1
        return self.sem

    def after(self, name, i=0):
        return (i + self.lead) * len(self.names) + self.names.index(name) + 1


class Kit:

    def __init__(self, nc, tag, ctx):
        self.nc, self.tag, self.ctx = nc, tag, ctx

    def sb(self, name, shape, dt=F32):
        return self.ctx.enter_context(self.nc.sbuf_tensor(f"{self.tag}_{name}", shape, dt))

    def ps(self, name, shape, dt=F32):
        return self.ctx.enter_context(self.nc.psum_tensor(f"{self.tag}_{name}", shape, dt))

    def sem(self, name):
        return self.ctx.enter_context(self.nc.semaphore(f"{self.tag}_{name}"))

    def steps(self, name, names, lead=1):
        return Steps(self.sem(name), names, lead)


def weight_columns(w, col, n):
    return w[:, ds(col, n)].rearrange("(k p) n -> p k n", p=P)


def phase_norm(nc, x, table_rows, ident_d, hT, table, ident):
    with ExitStack() as ctx:
        k = Kit(nc, "norm", ctx)
        xt = [k.sb(f"xt{u}", [P, D]) for u in range(2)]
        xn = [k.sb(f"xn{u}", [P, D]) for u in range(2)]
        junk = k.sb("junk", [P, D])
        rows = k.sb("rows", [N_ROWS, P])
        stat = [k.sb(f"stat{u}", [P, 3]) for u in range(2)]
        pt = [k.ps(f"pt{u}", [P, KT, P]) for u in range(2)]
        prow = k.ps("prow", [P, HALF])
        x_in = [k.sem(f"x_in{u}") for u in range(2)]
        rows_in = k.sem("rows_in")
        ident_in = k.sem("ident_in")
        table_t = k.sem("table_t")
        table_ok = k.sem("table_ok")
        A = k.steps("act", ["squares", "root"], 2)
        V = k.steps("dve", ["mean", "rstd", "scaled", "hT"], 2)
        M = k.steps("pe", ["turned"])
        block = ctx.enter_context(nc.Block())

        @block.sync
        def _(sp):
            sp.dma_start(ident[:, :], ident_d).then_inc(ident_in, 16)
            for row, src in table_rows:
                n = src.shape[0]
                sp.dma_start(rows[row:row + n, :], src).then_inc(rows_in, 16)
            with sp.Fori(0, NT // 2) as i:
                for u in range(2):
                    sp.wait_ge(A.sem, A.after("squares", 2 * i + u - 2))
                    sp.wait_ge(V.sem, V.after("scaled", 2 * i + u - 2))
                    sp.dma_start(xt[u][:, :], x[ds((2 * i + u) * P, P), :]).then_inc(x_in[u], 16)

        @block.scalar
        def _(act):
            A.start(act)
            with act.Fori(0, NT // 2) as i:
                for u in range(2):
                    n = 2 * i + u
                    act.wait_ge(x_in[u], 16 * i + 16)
                    act.wait_ge(V.sem, V.after("scaled", n - 2))
                    act.wait_ge(A.sem, A.after("squares", n - 1))
                    act.activation(junk[:, :], xt[u][:, :], ACT.Square,
                                   accum_out=stat[u][:, 0:1]).then_inc(A.mark("squares"), 1)
                    act.wait_ge(V.sem, V.after("mean", n))
                    act.activation(stat[u][:, 2:3], stat[u][:, 1:2], ACT.Sqrt).then_inc(A.mark("root"), 1)

        @block.vector
        def _(dve):
            V.start(dve)
            dve.wait_ge(table_t, 1)
            dve.tensor_copy(table[:, :], prow[:, 0:N_ROWS]).then_inc(table_ok, 1)
            dve.wait_ge(table_ok, 1)
            with dve.Fori(0, NT // 2) as i:
                for u in range(2):
                    n = 2 * i + u
                    dve.wait_ge(A.sem, A.after("squares", n))
                    dve.tensor_scalar(stat[u][:, 1:2], stat[u][:, 0:1], 1.0 / D, RMS_EPS, ALU.mult,
                                      ALU.add).then_inc(V.mark("mean"), 1)
                    dve.wait_ge(A.sem, A.after("root", n))
                    dve.reciprocal(stat[u][:, 2:3], stat[u][:, 2:3]).then_inc(V.mark("rstd"), 1)
                    dve.wait_ge(V.sem, V.after("rstd", n))
                    dve.tensor_scalar(xn[u][:, :], xt[u][:, :], stat[u][:, 2:3], None,
                                      ALU.mult).then_inc(V.mark("scaled"), 1)
                    dve.wait_ge(M.sem, M.after("turned", n))
                    nm = table[:, 0:KT].unsqueeze(2).to_broadcast([P, KT, P])
                    dve.tensor_tensor(hT[:, :, ds(n * P, P)], pt[u][:, :, :], nm,
                                      ALU.mult).then_inc(V.mark("hT"), 1)

        @block.tensor
        def _(pe):
            M.start(pe)
            pe.wait_ge(ident_in, 16)
            pe.wait_ge(rows_in, 16 * len(table_rows))
            pe.transpose(prow[:, 0:N_ROWS], rows[:, :], ident[0:N_ROWS, 0:N_ROWS]).then_inc(table_t, 1)
            with pe.Fori(0, NT // 2) as i:
                for u in range(2):
                    n = 2 * i + u
                    pe.wait_ge(V.sem, V.after("scaled", n))
                    for kt in range(KT):
                        mm = pe.transpose(pt[u][:, kt, :], xn[u][:, kt * P:(kt + 1) * P], ident[:, :])
                    mm.then_inc(M.mark("turned"), 1)


def phase_rwkv(nc, w_in, w_decay2, a2, g2, cd, hT, table, ident, ya_d, z_channel, z_token):
    with ExitStack() as ctx:
        k = Kit(nc, "rwkv", ctx)
        one_bd = k.sb("ones_bd", [P, P])
        gmask = k.sb("gmask", [P, 2 * P])
        lmask = k.sb("lmask", [P, LEVELS, P])
        l1up = k.sb("l1up", [P, P])
        running = k.sb("running", [P, T])
        lo = k.sb("lo", [P, 2, T])
        lom = k.sb("lom", [P, 2])
        wt = k.sb("wt", [P, 3, KT, P])
        lw = k.sb("lw", [P, 3, P])
        prm = k.sb("prm", [P, N_PAIR])
        omp = k.sb("omp", [P, N_PAIR])
        r, kx, v, icl, cs, pw, pinv, kk, sq, rn = (
            k.sb(n, [P, T]) for n in ("r", "k", "v", "icl", "cs", "pw", "pinv", "kk", "sq", "rn"))
        sig = pinv
        bonus, gate, Y = v, cs, kk
        ST = k.sb("ST", [P, NCH, 7, CH])
        BD = k.sb("BD", [P, QC, 6, P])
        G = k.sb("G", [P, QC, 4, P])
        TM = k.sb("TM", [P, QC, 5, P])
        Tt = k.sb("Tt", [P, QC, P])
        Nt = k.sb("Nt", [P, QC, P])
        X = k.sb("X", [P, QC, P])
        UT = k.sb("UT", [P, QC, 2, P])
        ET = X
        RH = k.sb("RH", [P, QC, CH])
        S = k.sb("S", [P, 2, P])
        y_out = k.sb("y_out", [P, T])
        side_w = [k.sb(f"side_w{u}", [P, KT, P]) for u in range(2)]
        side_z = [k.sb(f"side_z{u}", [P, HALF]) for u in range(2)]
        pp = k.ps("pp", [P, 8, HALF])

        y_stored = k.sem("y_stored")
        side_w_in = [k.sem(f"side_w_in{u}") for u in range(2)]
        side_mm = k.sem("side_mm")
        side_out = k.sem("side_out")
        side_stored = [k.sem(f"side_stored{u}") for u in range(2)]
        const_in = k.sem("const_in")
        lora_w_in = k.sem("lora_w_in")
        w_in_s = k.sem("w_in_s")
        cleared = k.sem("cleared")
        lora_mm = k.sem("lora_mm")
        lora_act = k.sem("lora_act")
        lora_dve = k.sem("lora_dve")
        PM = k.steps("pe_pair", ["w", "a", "k", "r", "kk", "v", "rk", "g", "mean", "var"])
        PA = k.steps("act_pair", ["sig", "icl", "k0", "P", "Pinv", "r0", "root", "v0", "V", "gate", "yc2", "yroot"])
        PV = k.steps("dve_pair", ["prm", "omp", "cs", "k", "kk", "kk2", "ka", "kf", "r", "rk2", "rn", "rp",
                                  "kn", "at0", "at1", "b", "bt", "kt", "rt", "Bh", "Kh", "v", "bonus", "S0",
                                  "Yc", "Yv", "Yp", "Yn", "Yl", "Yb", "Yg"])
        CM = k.steps("pe_chunk", ["gram", "X0", "turn", "X1", "T1", "N1", "Z0", "X2", "T2", "N2", "X3", "T3", "N3",
                                  "X4", "T4", "N4", "X5", "N5", "UT", "E", "RH", "S0", "S1", "S2", "S3", "Y"])
        CA = k.steps("act_chunk", ["bd0", "bd1", "TM", "Z0", "UT0", "UT1", "RH", "Y"])
        CV = k.steps("dve_chunk", ["G0", "G1", "G2", "G3", "X0", "T0", "N0m", "N0", "X1", "T1", "N1",
                                   "X2", "T2", "N2", "X3", "T3", "N3", "X4", "T4", "N4", "X5", "N5",
                                   "diag", "E", "S0", "S1", "S2", "S3"])
        block = ctx.enter_context(nc.Block())
        mu = ROWS["mu_a"][0]
        first = ROWS["w_decay0"][0]

        def chunked(ap):
            return ap.rearrange("p (c t) -> p c t", t=CH)

        def bank2(b):
            return pp[:, b:b + 2, :].rearrange("p a n -> p (a n)")

        def bank4(b):
            return pp[:, b, :].rearrange("p (u n) -> p u n", u=QC)

        def over_chunks(ap):
            return ap.unsqueeze(1).to_broadcast([P, QC, P])

        SIDE_UNITS = 2 * NQ + 2

        @block.sync
        def _(sp):
            for dst, src in ((one_bd[:, :], cd["ones_bd"]), (gmask[:, :], cd["gram_mask"]),
                             (lmask[:, :, :].rearrange("p l n -> p (l n)"), cd["level_mask"]),
                             (l1up[:, :], cd["level1_up"]), (running[:, :], cd["running"])):
                sp.dma_start(dst, src).then_inc(const_in, 16)
            for j in range(2):
                sp.dma_start(wt[:, j, :, :], weight_columns(w_in, 3 * A_WIDTH + j * P, P)).then_inc(lora_w_in, 16)
            sp.wait_ge(cleared, 3)
            sp.wait_ge(lora_mm, 2)

            def weights(p):
                sp.wait_ge(PM.sem, PM.after("g", p - 1))
                sp.dma_start(lw[0:64, 0, :], w_decay2[:, ds(p * P, P)]).then_inc(w_in_s, 16)
                sp.dma_start(lw[64:128, 1, :], a2[:, ds(p * P, P)]).then_inc(w_in_s, 16)
                sp.dma_start(lw[:, 2, :], g2[:, ds(p * P, P)]).then_inc(w_in_s, 16)
                for j in range(3):
                    sp.dma_start(wt[:, j, :, :], weight_columns(w_in, j * A_WIDTH + p * P, P)).then_inc(w_in_s, 16)

            def side_weights(slot, col):
                sp.dma_start(side_w[slot][:, :, :], weight_columns(w_in, col, P)).then_inc(side_w_in[slot], 16)

            def loop_column(p, q):
                return COL_G + q * D + p * P if q < 3 else COL_C + p * P

            def pair(p, last):
                def store(j, dst):
                    z = side_z[j % 2][:, :]
                    sp.wait_ge(side_out, SIDE_UNITS * p + j + 2)
                    if len(dst.shape) == 3:
                        z = z.rearrange("p (t n) -> p t n", t=4)
                    sp.dma_start(dst, z).then_inc(side_stored[j % 2], 16)

                def by_token(h):
                    return z_token[h * HALF:(h + 1) * HALF, ds(p * P, P)].rearrange("(t p) n -> p t n", p=P)

                store(0, by_token(0))
                if not last:
                    weights(p + 1)
                for q in range(NQ):
                    for h in range(2):
                        store(1 + 2 * q + h, z_channel[ds((q * KT + p) * P, P), h * HALF:(h + 1) * HALF])
                    if q < NQ - 1:
                        side_weights(0, loop_column(p, q + 1))
                    elif not last:
                        side_weights(0, loop_column(p + 1, 0))
                store(SIDE_UNITS - 1, by_token(1))
                if not last:
                    side_weights(1, COL_C + C_WIDTH + (p + 1) * P)
                sp.wait_ge(PV.sem, PV.after("Yg", p))
                sp.dma_start(ya_d[ds(p * P, P), :], y_out[:, :]).then_inc(y_stored, 16)

            weights(0)
            side_weights(1, COL_C + C_WIDTH)
            side_weights(0, loop_column(0, 0))
            with sp.Fori(0, PAIRS - 1) as p:
                pair(p, False)
            pair(PAIRS - 1, True)
            for u in range(2):
                sp.wait_ge(side_stored[u], 16 * (PAIRS * SIDE_UNITS // 2 + 1))
            sp.wait_ge(y_stored, 16 * (PAIRS + 1))

        def project(bank, w):
            for h in range(2):
                for kt in range(KT):
                    mm = nc.tensor.matmul(pp[:, bank + h, :], w[:, kt, :], hT[:, kt, h * HALF:(h + 1) * HALF],
                                          start=kt == 0, stop=kt == KT - 1)
            return mm

        def across(bank, lhsT, rhs):
            for h in range(2):
                mm = nc.tensor.matmul(pp[:, bank + h, :], lhsT, rhs[:, h * HALF:(h + 1) * HALF], start=True, stop=True)
            return mm

        @block.tensor
        def _(pe):
            PM.start(pe)
            CM.start(pe)
            pe.wait_ge(lora_w_in, 32)
            project(0, wt[:, 0, :, :]).then_inc(lora_mm, 1)
            project(2, wt[:, 1, :, :]).then_inc(lora_mm, 1)
            pe.wait_ge(const_in, 5 * 16)
            pe.wait_ge(lora_act, 4)
            pe.wait_ge(lora_dve, 3)
            with pe.Fori(0, PAIRS) as p:
                def side_token(j, h):
                    pe.wait_ge(side_w_in[1], 16 * p + 16)
                    pe.wait_ge(side_out, SIDE_UNITS * p + j + 1)
                    for t in range(4):
                        for kt in range(KT):
                            mm = pe.matmul(pp[:, 7, t * P:(t + 1) * P], hT[:, kt, (4 * h + t) * P:(4 * h + t + 1) * P],
                                           side_w[1][:, kt, :], start=kt == 0, stop=kt == KT - 1)
                    mm.then_inc(side_mm, 1)

                pe.wait_ge(w_in_s, 96 * p + 96)
                pe.wait_ge(PV.sem, PV.after("Yv", p - 1))
                across(0, lw[:, 0, :], lo[:, 0, :]).then_inc(PM.mark("w"), 1)
                across(2, lw[:, 1, :], lo[:, 0, :]).then_inc(PM.mark("a"), 1)
                project(4, wt[:, 1, :, :]).then_inc(PM.mark("k"), 1)
                pe.wait_ge(PA.sem, PA.after("icl", p))
                project(0, wt[:, 0, :, :]).then_inc(PM.mark("r"), 1)
                pe.wait_ge(PV.sem, PV.after("kk2", p))
                across(4, one_bd[:, :], sq).then_inc(PM.mark("kk"), 1)
                project(2, wt[:, 2, :, :]).then_inc(PM.mark("v"), 1)
                pe.wait_ge(PV.sem, PV.after("rk2", p))
                across(0, one_bd[:, :], rn).then_inc(PM.mark("rk"), 1)
                side_token(0, 0)
                pe.wait_ge(PV.sem, PV.after("v", p))
                across(2, lw[:, 2, :], lo[:, 1, :]).then_inc(PM.mark("g"), 1)

                with pe.Fori(0, NQ) as q:
                    it = p * NQ + q

                    def side(first, last):
                        for m in range(first, last):
                            h, kt = m // KT, m % KT
                            if m == 0:
                                pe.wait_ge(side_w_in[0], 16 * it + 16)
                            if kt == 0:
                                pe.wait_ge(side_out, SIDE_UNITS * p + 2 * q + h + 2)
                            mm = pe.matmul(pp[:, 7, :], side_w[0][:, kt, :], hT[:, kt, h * HALF:(h + 1) * HALF],
                                           start=kt == 0, stop=kt == KT - 1)
                            if kt == KT - 1:
                                mm.then_inc(side_mm, 1)

                    pe.wait_ge(CA.sem, CA.after("bd1", it))
                    pe.wait_ge(CV.sem, CV.after("S3", it - 1))
                    for u in range(QC):
                        for j, half in ((4, 0), (5, 256)):
                            st = ST[:, ds(q * QC + u, 1), 0:2, :].rearrange("p c a t -> p (c a) t")
                            mm = pe.matmul(pp[:, u, half:half + 256].rearrange("p (a h t) -> p a h t", a=2, h=2),
                                           BD[:, u, j, :], st.unsqueeze(2).to_broadcast([P, 2, 2, CH]),
                                           start=True, stop=True)
                    mm.then_inc(CM.mark("gram"), 1)
                    side(0, 3)
                    pe.wait_ge(CV.sem, CV.after("G3", it))
                    for u in range(QC):
                        mm = pe.matmul(bank4(4)[:, u, :], G[:, u, 1, :], ident[:, :], start=True, stop=True)
                    mm.then_inc(CM.mark("X0"), 1)
                    for u in range(QC):
                        for j in range(4):
                            mm = pe.transpose(pp[:, u, j * P:(j + 1) * P], BD[:, u, j, :], ident[:, :])
                    mm.then_inc(CM.mark("turn"), 1)
                    for lv in range(1, LEVELS):
                        pe.wait_ge(CV.sem, CV.after(f"T{lv - 1}", it))
                        for u in range(QC):
                            mm = pe.matmul(bank4(4)[:, u, :], G[:, u, 1, :], Tt[:, u, :], start=True, stop=True)
                        mm.then_inc(CM.mark(f"X{lv}"), 1)
                        side(2 * lv + 1, 2 * lv + 2)
                        pe.wait_ge(CV.sem, CV.after(f"X{lv}", it))
                        if lv < LEVELS - 1:
                            for u in range(QC):
                                mm = pe.matmul(bank4(5)[:, u, :], Nt[:, u, :], X[:, u, :], start=True, stop=True)
                            mm.then_inc(CM.mark(f"T{lv}"), 1)
                        for u in range(QC):
                            mm = pe.matmul(bank4(6)[:, u, :], X[:, u, :], Nt[:, u, :], start=True, stop=True)
                        mm.then_inc(CM.mark(f"N{lv}"), 1)
                        if lv == 1:
                            pe.wait_ge(CA.sem, CA.after("TM", it))
                            for u in range(QC):
                                mm = pe.matmul(bank4(0)[:, u, :], G[:, u, 3, :], TM[:, u, 4, :], start=True, stop=True)
                            mm.then_inc(CM.mark("Z0"), 1)
                        side(2 * lv + 2, 2 * lv + 3)
                    pe.wait_ge(CV.sem, CV.after("N5", it))
                    pe.wait_ge(CA.sem, CA.after("Z0", it))
                    for u in range(QC):
                        mm = pe.matmul(pp[:, u // 2, (u % 2) * 256:(u % 2) * 256 + 256], Nt[:, u, :],
                                       TM[:, u, 0:2, :].rearrange("p a n -> p (a n)"), start=True, stop=True)
                    mm.then_inc(CM.mark("UT"), 1)
                    side(13, 16)
                    pe.wait_ge(CA.sem, CA.after("UT1", it))
                    for u in range(QC):
                        mm = pe.matmul(bank4(2)[:, u, :], UT[:, u, 1, :], TM[:, u, 2, :], start=True, stop=True)
                    mm.then_inc(CM.mark("E"), 1)
                    for u in range(QC):
                        out = pp[:, 3, u * CH:(u + 1) * CH]
                        pe.matmul(out, UT[:, u, 1, :], G[:, u, 0, 0:CH], start=True, stop=False)
                        pe.matmul(out, UT[:, u, 1, :], G[:, u, 0, CH:P], start=False, stop=False)
                        mm = pe.matmul(out, ident[:, :], ST[:, ds(q * QC + u, 1), 0, :].rearrange("p c t -> p (c t)"),
                                       start=False, stop=True)
                    mm.then_inc(CM.mark("RH"), 1)
                    for u in range(QC):
                        out = pp[:, 5 + u % 2, 0:P]
                        pe.matmul(out, TM[:, u, 2, :], UT[:, u, 0, :], start=True, stop=False)
                        pe.matmul(out, TM[:, u, 3, :], TM[:, u, 4, :], start=False, stop=False)
                        if u == 0:
                            pe.wait_ge(CV.sem, CV.after("E", it))
                        else:
                            pe.wait_ge(CV.sem, CV.after(f"S{u - 1}", it))
                        pe.matmul(out, ET[:, u, :], S[:, u % 2, :], start=False, stop=True).then_inc(CM.mark(f"S{u}"), 1)
                        if u == 0:
                            pe.wait_ge(CA.sem, CA.after("RH", it))
                        out = pp[:, 3, (QC + u) * CH:(QC + u + 1) * CH]
                        pe.matmul(out, S[:, u % 2, :], RH[:, u, :], start=True, stop=False)
                        for lhsT, j in ((UT[:, u, 0, :], 0), (TM[:, u, 4, :], 2)):
                            for h in range(2):
                                mm = pe.matmul(out, lhsT, G[:, u, j, h * CH:(h + 1) * CH],
                                               start=False, stop=j == 2 and h == 1)
                    mm.then_inc(CM.mark("Y"), 1)

                pe.wait_ge(CA.sem, CA.after("Y", p * NQ + NQ - 1))
                across(0, one_bd[:, :], Y).then_inc(PM.mark("mean"), 1)
                side_token(SIDE_UNITS - 1, 1)
                pe.wait_ge(PA.sem, PA.after("yc2", p))
                across(2, one_bd[:, :], sq).then_inc(PM.mark("var"), 1)

        @block.scalar
        def _(act):
            PA.start(act)
            CA.start(act)
            act.wait_ge(lora_dve, 1)
            for j in range(2):
                act.wait_ge(lora_mm, j + 1)
                act.activation(lo[:, j, :], bank2(2 * j), ACT.Copy, scale=lom[:, j:j + 1]).then_inc(lora_act, 1)
            act.wait_ge(lora_dve, 3)
            act.activation(lo[0:64, 0, :], lo[0:64, 0, :], ACT.Tanh).then_inc(lora_act, 1)
            act.activation(lo[:, 1, :], lo[:, 1, :], ACT.Sigmoid).then_inc(lora_act, 1)
            with act.Fori(0, PAIRS) as p:
                act.wait_ge(PV.sem, PV.after("omp", p))

                def shifted(name, dst, bank, col):
                    act.wait_ge(PM.sem, PM.after(name, p))
                    act.activation(dst[:, :], bank2(bank), ACT.Copy, scale=omp[:, col:col + 1]).then_inc(PA.mark(name + "0"), 1)

                def side_evacuate(j, u):
                    n = SIDE_UNITS * p + j
                    act.wait_ge(side_mm, n + 1)
                    act.wait_ge(side_stored[u], 8 * (n - u) + 16)
                    act.activation(side_z[u][:, :], pp[:, 7, :], ACT.Copy).then_inc(side_out, 1)

                act.wait_ge(PM.sem, PM.after("w", p))
                act.activation(sig[:, :], bank2(0), ACT.Sigmoid, bias=prm[:, W0:W0 + 1]).then_inc(PA.mark("sig"), 1)
                act.wait_ge(PM.sem, PM.after("a", p))
                act.activation(icl[:, :], bank2(2), ACT.Sigmoid, bias=prm[:, A0:A0 + 1]).then_inc(PA.mark("icl"), 1)
                shifted("k", kx, 4, MU_K)
                act.wait_ge(PV.sem, PV.after("cs", p))
                act.activation(pw[:, :], cs[:, :], ACT.Exp, scale=-DECAY_SCALE).then_inc(PA.mark("P"), 1)
                act.activation(pinv[:, :], cs[:, :], ACT.Exp, scale=DECAY_SCALE).then_inc(PA.mark("Pinv"), 1)
                shifted("r", r, 0, MU_R)
                act.wait_ge(PV.sem, PV.after("rn", p))
                act.activation(sq[:, :], sq[:, :], ACT.Sqrt).then_inc(PA.mark("root"), 1)
                shifted("v", v, 2, MU_V)
                act.wait_ge(PV.sem, PV.after("v", p))
                act.activation(ST[:, :, 4, :], chunked(v[:, :]), ACT.Copy).then_inc(PA.mark("V"), 1)
                side_evacuate(0, 0)
                act.wait_ge(PM.sem, PM.after("g", p))
                act.wait_ge(PA.sem, PA.after("Pinv", p))
                act.activation(gate[:, :], bank2(2), ACT.Copy).then_inc(PA.mark("gate"), 1)

                with act.Fori(0, NQ) as q:
                    it = p * NQ + q
                    act.wait_ge(PV.sem, PV.after("S0", p))
                    act.wait_ge(PA.sem, PA.after("V", p))
                    act.wait_ge(CM.sem, CM.after("turn", it - 1))
                    for h in range(2):
                        rows = slice(h * CH, (h + 1) * CH)
                        act.activation(BD[rows, :, :, h * CH:(h + 1) * CH], ST[rows, ds(q * QC, QC), 1:7, :],
                                       ACT.Copy).then_inc(CA.mark(f"bd{h}"), 1)
                    act.wait_ge(CM.sem, CM.after("turn", it))
                    act.activation(TM[:, :, 1:5, :].rearrange("p u a n -> p u (a n)"), pp[:, 0:4, :],
                                   ACT.Copy).then_inc(CA.mark("TM"), 1)
                    act.wait_ge(CM.sem, CM.after("Z0", it))
                    act.activation(TM[:, :, 0, :], bank4(0), ACT.Copy).then_inc(CA.mark("Z0"), 1)
                    side_evacuate(1 + 2 * q, 1)
                    act.wait_ge(CM.sem, CM.after("UT", it))
                    for b in range(2):
                        act.activation(UT[:, 2 * b:2 * b + 2, :, :].rearrange("p u a n -> p (u a n)"), pp[:, b, :],
                                       ACT.Copy).then_inc(CA.mark(f"UT{b}"), 1)
                    side_evacuate(2 + 2 * q, 0)
                    act.wait_ge(CM.sem, CM.after("RH", it))
                    act.activation(RH[:, :, :].rearrange("p u t -> p (u t)"), pp[:, 3, 0:QC * CH],
                                   ACT.Copy).then_inc(CA.mark("RH"), 1)
                    act.wait_ge(CM.sem, CM.after("Y", it))
                    act.activation(Y[:, ds(q * QC * CH, QC * CH)], pp[:, 3, QC * CH:2 * QC * CH], ACT.Copy).then_inc(CA.mark("Y"), 1)

                act.wait_ge(PV.sem, PV.after("Yc", p))
                act.activation(sq[:, :], Y[:, :], ACT.Square).then_inc(PA.mark("yc2"), 1)
                side_evacuate(SIDE_UNITS - 1, 1)
                act.wait_ge(PV.sem, PV.after("Yv", p))
                act.activation(rn[:, :], rn[:, :], ACT.Sqrt).then_inc(PA.mark("yroot"), 1)

        @block.gpsimd
        def _(pool):
            pool.memset(lw[:, :, :], 0.0).then_inc(cleared, 1)
            pool.memset(BD[:, :, :, :], 0.0).then_inc(cleared, 1)
            pool.memset(S[:, :, :], 0.0).then_inc(cleared, 1)
            pool.sem_inc(side_out, 1)
            pool.sem_inc(y_stored, 16)
            for u in range(2):
                pool.sem_inc(side_stored[u], 16)

        @block.vector
        def _(dve):
            PV.start(dve)
            CV.start(dve)
            dve.tensor_scalar(lom[:, :], table[:, mu + 24:mu + 26], -1.0, 1.0, ALU.mult, ALU.add).then_inc(lora_dve, 1)
            for j in range(2):
                dve.wait_ge(lora_act, j + 1)
                dve.scalar_tensor_tensor(out=lo[:, j, 1:T], in0=bank2(2 * j)[:, 0:T - 1],
                                         scalar=table[:, mu + 24 + j:mu + 25 + j], in1=lo[:, j, 1:T],
                                         op0=ALU.mult, op1=ALU.add).then_inc(lora_dve, 1)
            dve.wait_ge(cleared, 3)
            dve.wait_ge(const_in, 5 * 16)
            with dve.Fori(0, PAIRS) as p:
                def mine(name):
                    dve.wait_ge(PV.sem, PV.after(name, p))

                columns = table[:, first:first + 8 * N_PAIR].rearrange("p (a b) -> p a b", b=8)
                dve.wait_ge(PV.sem, PV.after("Yg", p - 1))
                dve.tensor_copy(prm[:, :].unsqueeze(2), columns[:, :, ds(p, 1)]).then_inc(PV.mark("prm"), 1)
                mine("prm")
                dve.tensor_scalar(omp[:, :], prm[:, :], -1.0, 1.0, ALU.mult, ALU.add).then_inc(PV.mark("omp"), 1)

                def shift(name, dst, bank, col):
                    dve.wait_ge(PA.sem, PA.after(name + "0", p))
                    dve.scalar_tensor_tensor(out=dst[:, 1:T], in0=bank2(bank)[:, 0:T - 1], scalar=prm[:, col:col + 1],
                                             in1=dst[:, 1:T], op0=ALU.mult, op1=ALU.add).then_inc(PV.mark(name), 1)

                dve.wait_ge(PA.sem, PA.after("sig", p))
                dve.tensor_tensor_scan(cs[:, :], running[:, :], sig[:, :], 0.0, ALU.mult, ALU.add).then_inc(PV.mark("cs"), 1)
                shift("k", kx, 4, MU_K)
                mine("k")
                dve.tensor_scalar(kk[:, :], kx[:, :], prm[:, K_K:K_K + 1], None, ALU.mult).then_inc(PV.mark("kk"), 1)
                mine("kk")
                dve.tensor_tensor(sq[:, :], kk[:, :], kk[:, :], ALU.mult).then_inc(PV.mark("kk2"), 1)
                dve.wait_ge(PA.sem, PA.after("icl", p))
                dve.tensor_scalar(rn[:, :], icl[:, :], prm[:, K_A:K_A + 1], omp[:, K_A:K_A + 1],
                                  ALU.mult, ALU.add).then_inc(PV.mark("ka"), 1)
                mine("ka")
                dve.tensor_tensor(kx[:, :], kx[:, :], rn[:, :], ALU.mult).then_inc(PV.mark("kf"), 1)
                shift("r", r, 0, MU_R)
                mine("r")
                dve.scalar_tensor_tensor(out=rn[:, :], in0=r[:, :], scalar=prm[:, R_K:R_K + 1], in1=kx[:, :],
                                         op0=ALU.mult, op1=ALU.mult).then_inc(PV.mark("rk2"), 1)
                dve.wait_ge(PM.sem, PM.after("kk", p))
                dve.tensor_scalar(sq[:, :], bank2(4), 1e-24, None, ALU.max).then_inc(PV.mark("rn"), 1)
                dve.wait_ge(PA.sem, PA.after("root", p))
                dve.reciprocal(sq[:, :], sq[:, :]).then_inc(PV.mark("rp"), 1)
                mine("rp")
                dve.tensor_tensor(kk[:, :], kk[:, :], sq[:, :], ALU.mult).then_inc(PV.mark("kn"), 1)
                mine("kn")
                dve.wait_ge(PA.sem, PA.after("Pinv", p))
                dve.scalar_tensor_tensor(out=ST[:, :, 1, 1:CH], in0=chunked(kk[:, :])[:, :, 1:CH], scalar=-1.0,
                                         in1=chunked(pw[:, :])[:, :, 0:CH - 1], op0=ALU.mult,
                                         op1=ALU.mult).then_inc(PV.mark("at0"), 1)
                dve.tensor_scalar(ST[:, :, 1, 0:1], chunked(kk[:, :])[:, :, 0:1], -1.0, None,
                                  ALU.mult).then_inc(PV.mark("at1"), 1)
                dve.tensor_tensor(icl[:, :], kk[:, :], icl[:, :], ALU.mult).then_inc(PV.mark("b"), 1)
                mine("b")
                dve.tensor_tensor(ST[:, :, 5, :], chunked(icl[:, :]), chunked(pinv[:, :]), ALU.mult).then_inc(PV.mark("bt"), 1)
                dve.tensor_tensor(ST[:, :, 6, :], chunked(kx[:, :]), chunked(pinv[:, :]), ALU.mult).then_inc(PV.mark("kt"), 1)
                dve.tensor_tensor(ST[:, :, 0, :], chunked(r[:, :]), chunked(pw[:, :]), ALU.mult).then_inc(PV.mark("rt"), 1)
                mine("kt")
                last = chunked(pw[:, :])[:, :, CH - 1:CH].to_broadcast([P, NCH, CH])
                dve.tensor_tensor(ST[:, :, 2, :], ST[:, :, 5, :], last, ALU.mult).then_inc(PV.mark("Bh"), 1)
                dve.tensor_tensor(ST[:, :, 3, :], ST[:, :, 6, :], last, ALU.mult).then_inc(PV.mark("Kh"), 1)
                shift("v", v, 2, MU_V)
                dve.wait_ge(PM.sem, PM.after("rk", p))
                dve.wait_ge(PA.sem, PA.after("V", p))
                dve.tensor_tensor(bonus[:, :], bank2(0), v[:, :], ALU.mult).then_inc(PV.mark("bonus"), 1)
                dve.memset(S[:, 0, :], 0.0).then_inc(PV.mark("S0"), 1)

                with dve.Fori(0, NQ) as q:
                    it = p * NQ + q

                    def own(name):
                        dve.wait_ge(CV.sem, CV.after(name, it))

                    dve.wait_ge(CM.sem, CM.after("gram", it))
                    for u in range(QC):
                        dve.tensor_tensor(G[:, u, :, :].rearrange("p (b a) n -> p b (a n)", b=2),
                                          pp[:, u, :].rearrange("p (b n) -> p b n", b=2),
                                          gmask[:, :].unsqueeze(1).to_broadcast([P, 2, 2 * P]), ALU.mult).then_inc(CV.mark(f"G{u}"), 1)
                    dve.wait_ge(CM.sem, CM.after("X0", it))
                    dve.tensor_tensor(Tt[:, :, :], bank4(4), over_chunks(lmask[:, 0, :]), ALU.mult).then_inc(CV.mark("X0"), 1)
                    own("X0")
                    dve.tensor_tensor(Tt[:, :, :], Tt[:, :, :], over_chunks(ident[:, :]), ALU.add).then_inc(CV.mark("T0"), 1)
                    dve.tensor_tensor(Nt[:, :, :], G[:, :, 1, :], over_chunks(l1up[:, :]), ALU.mult).then_inc(CV.mark("N0m"), 1)
                    own("N0m")
                    dve.tensor_tensor(Nt[:, :, :], Nt[:, :, :], over_chunks(ident[:, :]), ALU.add).then_inc(CV.mark("N0"), 1)
                    for lv in range(1, LEVELS):
                        own(f"N{lv - 1}")
                        dve.wait_ge(CM.sem, CM.after(f"X{lv}", it))
                        dve.tensor_tensor(X[:, :, :], bank4(4), over_chunks(lmask[:, lv, :]), ALU.mult).then_inc(CV.mark(f"X{lv}"), 1)
                        if lv < LEVELS - 1:
                            dve.wait_ge(CM.sem, CM.after(f"T{lv}", it))
                            dve.tensor_tensor(Tt[:, :, :], Tt[:, :, :], bank4(5), ALU.add).then_inc(CV.mark(f"T{lv}"), 1)
                        dve.wait_ge(CM.sem, CM.after(f"N{lv}", it))
                        dve.tensor_tensor(Nt[:, :, :], Nt[:, :, :], bank4(6), ALU.add).then_inc(CV.mark(f"N{lv}"), 1)
                    last = chunked(pw[:, :])[:, ds(q * QC, QC), CH - 1:CH].to_broadcast([P, QC, P])
                    dve.tensor_tensor(ET[:, :, :], over_chunks(ident[:, :]), last, ALU.mult).then_inc(CV.mark("diag"), 1)
                    own("diag")
                    dve.wait_ge(CM.sem, CM.after("E", it))
                    dve.tensor_tensor(ET[:, :, :], ET[:, :, :], bank4(2), ALU.add).then_inc(CV.mark("E"), 1)
                    for u in range(QC):
                        dve.wait_ge(CM.sem, CM.after(f"S{u}", it))
                        dve.tensor_copy(S[:, (u + 1) % 2, :], pp[:, 5 + u % 2, 0:P]).then_inc(CV.mark(f"S{u}"), 1)

                dve.wait_ge(PM.sem, PM.after("mean", p))
                dve.scalar_tensor_tensor(out=Y[:, :], in0=bank2(0), scalar=-1.0 / HEAD, in1=Y[:, :], op0=ALU.mult,
                                         op1=ALU.add).then_inc(PV.mark("Yc"), 1)
                dve.wait_ge(PM.sem, PM.after("var", p))
                dve.tensor_scalar(rn[:, :], bank2(2), 1.0 / HEAD, GN_EPS, ALU.mult, ALU.add).then_inc(PV.mark("Yv"), 1)
                dve.wait_ge(PA.sem, PA.after("yroot", p))
                dve.reciprocal(rn[:, :], rn[:, :]).then_inc(PV.mark("Yp"), 1)
                mine("Yp")
                dve.tensor_tensor(Y[:, :], Y[:, :], rn[:, :], ALU.mult).then_inc(PV.mark("Yn"), 1)
                mine("Yn")
                dve.tensor_scalar(Y[:, :], Y[:, :], prm[:, LNX_W:LNX_W + 1], prm[:, LNX_B:LNX_B + 1],
                                  ALU.mult, ALU.add).then_inc(PV.mark("Yl"), 1)
                mine("Yl")
                dve.tensor_tensor(Y[:, :], Y[:, :], bonus[:, :], ALU.add).then_inc(PV.mark("Yb"), 1)
                mine("Yb")
                dve.wait_ge(y_stored, 16 * p + 16)
                dve.tensor_tensor(y_out[:, :], Y[:, :], gate[:, :], ALU.mult).then_inc(PV.mark("Yg"), 1)


def phase_qkv(nc, w_in, cd, hT, QK, VS, y_extra, ya_d, yA):
    with ExitStack() as ctx:
        k = Kit(nc, "qkv", ctx)
        w = [k.sb(f"w{u}", [P, KT, P]) for u in range(2)]
        wv = k.sb("wv", [P, KT, B_WIDTH])
        cos = k.sb("cos", [P, T])
        sin = k.sb("sin", [P, T])
        swap = k.sb("swap", [P, P])
        raw = [k.sb(f"raw{u}", [P, T]) for u in range(2)]
        t2 = [k.sb(f"t2{u}", [P, T]) for u in range(2)]
        pp = k.ps("pp", [P, 8, HALF])
        w_s = [k.sem(f"w_s{u}") for u in range(2)]
        wv_s = k.sem("wv_s")
        const_in = k.sem("const_in")
        proj_done = [k.sem(f"proj_done{u}") for u in range(2)]
        swap_done = [k.sem(f"swap_done{u}") for u in range(2)]
        A = k.steps("act", ["raw"], 2)
        V = k.steps("dve", ["sin", "cos", "rot"], 2)
        zero = k.sb("zero", [P, D])
        zero_set = k.sem("zero_set")
        ya_in = k.sem("ya_in")
        zeros_out = k.sem("zeros_out")
        values_mm = k.sem("values_mm")
        values_out = k.sem("values_out")
        NQK = 2 * B_WIDTH // P
        block = ctx.enter_context(nc.Block())

        def bank2(b):
            return pp[:, b:b + 2, :].rearrange("p a n -> p (a n)")

        @block.sync
        def _(sp):
            for dst, src in ((cos, "rope_cos"), (sin, "rope_sin"), (swap, "swap")):
                sp.dma_start(dst[:, :], cd[src]).then_inc(const_in, 16)
            with sp.Fori(0, NQK // 2) as i:
                for u in range(2):
                    n = 2 * i + u
                    sp.wait_ge(proj_done[u], i + 1)
                    sp.dma_start(w[u][:, :, :], weight_columns(w_in, COL_B + n * P, P)).then_inc(w_s[u], 16)
            sp.dma_start(wv[:, :, :], weight_columns(w_in, COL_B + 2 * B_WIDTH, B_WIDTH)).then_inc(wv_s, 16)
            sp.dma_start(yA[:, :, :], ya_d.rearrange("(k p) t -> p k t", p=P)).then_inc(ya_in, 16)
            sp.wait_ge(zero_set, 1)
            for b in range(MAX_EXTRA):
                sp.dma_start(y_extra[b * SLOTS:(b + 1) * SLOTS, :], zero[:, :]).then_inc(zeros_out, 16)
            sp.wait_ge(zeros_out, 16 * MAX_EXTRA)
            sp.wait_ge(ya_in, 16)

        @block.gpsimd
        def _(pool):
            pool.memset(zero[:, :], 0.0).then_inc(zero_set, 1)

        @block.tensor
        def _(pe):
            for u in range(2):
                pe.sem_inc(proj_done[u], 1)
            pe.wait_ge(const_in, 48)
            with pe.Fori(0, NQK // 2) as i:
                for u in range(2):
                    n = 2 * i + u
                    pe.wait_ge(w_s[u], 16 * i + 16)
                    pe.wait_ge(A.sem, A.after("raw", n - 2))
                    for h in range(2):
                        for kt in range(KT):
                            mm = pe.matmul(pp[:, 4 * u + h, :], w[u][:, kt, :], hT[:, kt, h * HALF:(h + 1) * HALF],
                                           start=kt == 0, stop=kt == KT - 1)
                    mm.then_inc(proj_done[u], 1)
                for u in range(2):
                    n = 2 * i + u
                    pe.wait_ge(A.sem, A.after("raw", n))
                    pe.wait_ge(V.sem, V.after("sin", n - 2))
                    for h in range(2):
                        mm = pe.matmul(pp[:, 4 * u + 2 + h, :], swap[:, :], raw[u][:, h * HALF:(h + 1) * HALF],
                                       start=True, stop=True)
                    mm.then_inc(swap_done[u], 1)
            pe.wait_ge(wv_s, 16)
            pe.wait_ge(V.sem, V.after("sin", NQK - 1))
            for n in range(24):
                if n >= 8:
                    pe.wait_ge(values_out, n - 7)
                for kt in range(KT):
                    mm = pe.matmul(pp[:, n % 8, 0:B_OUT], tile_tokens(hT[:, kt, :], n), wv[:, kt, n // 8 * B_OUT:(n // 8 + 1) * B_OUT],
                                   start=kt == 0, stop=kt == KT - 1)
                mm.then_inc(values_mm, 1)

        @block.scalar
        def _(act):
            A.start(act)
            with act.Fori(0, NQK // 2) as i:
                for u in range(2):
                    n = 2 * i + u
                    act.wait_ge(proj_done[u], i + 2)
                    act.wait_ge(V.sem, V.after("rot", n - 2))
                    act.activation(raw[u][:, :], bank2(4 * u), ACT.Copy).then_inc(A.mark("raw"), 1)
            for n in range(24):
                act.wait_ge(values_mm, n + 1)
                act.activation(VS[:, n, :], pp[:, n % 8, 0:B_OUT], ACT.Copy).then_inc(values_out, 1)

        @block.vector
        def _(dve):
            V.start(dve)
            dve.wait_ge(const_in, 48)
            with dve.Fori(0, NQK // 2) as i:
                for u in range(2):
                    n = 2 * i + u
                    dve.wait_ge(swap_done[u], i + 1)
                    dve.wait_ge(V.sem, V.after("rot", n - 2))
                    dve.tensor_tensor(t2[u][:, :], bank2(4 * u + 2), sin[:, :], ALU.mult).then_inc(V.mark("sin"), 1)
                    dve.tensor_tensor(raw[u][:, :], raw[u][:, :], cos[:, :], ALU.mult).then_inc(V.mark("cos"), 1)
                    dve.wait_ge(V.sem, V.after("cos", n))
                    dve.tensor_tensor(QK[:, ds(n, 1), :].rearrange("p a t -> p (a t)"), raw[u][:, :], t2[u][:, :],
                                      ALU.add).then_inc(V.mark("rot"), 1)


DILATION = (1, 4, 16)


def tile_tokens(ap, n):
    group, j = n // 8, n % 8
    if group == 0:
        return ap[:, j * P:(j + 1) * P]
    if group == 1:
        start = j // 4 * 4 * P + j % 4
        return ap[:, start:start + 4 * P - 3:4]
    return ap[:, j:j + 8 * P - 7:8]


def moving_tokens(ap, group, j, block=0):
    if group == 0:
        return ap[:, :, ds(j * P, P)].unsqueeze(2)
    if group == 1:
        return ap.rearrange("p a (n l r) -> p a r n l", n=2, r=4)[:, :, ds(j, 1), block, :]
    return ap.rearrange("p a (l r) -> p a r l", r=8)[:, :, ds(j, 1), :]


SEGMENTS = [(0, 0, 0, 1, 0), (0, 1, 0, 2, 0), (0, 2, 6, 2, 0), (1, 0, 4, 1, 0), (1, 0, 4, 2, 1), (2, 0, 8, 1, 0)]
OUT_W = B_OUT + 2 * B_GROUP_HEADS


def phase_attend(nc, cd, scratch, QK, VS, ident, yB):
    with ExitStack() as ctx:
        k = Kit(nc, "attn", ctx)
        H = B_GROUP_HEADS
        mask_two = k.sb("mask_two", [P, 2 * P])
        mask_pair = k.sb("mask_pair", [P, P])
        q = [k.sb(f"q{u}", [P, H, P]) for u in range(2)]
        sm = [k.sb(f"sm{u}", [P, H, 2 * P]) for u in range(2)]
        pT = [k.sb(f"pT{u}", [P, H, 2, P]) for u in range(2)]
        mx = [k.sb(f"mx{u}", [P, 3, H]) for u in range(2)]
        ob = [k.sb(f"ob{u}", [P, OUT_W]) for u in range(2)]
        cb = k.sb("cb", [P, 3, NT, OUT_W])
        cw = k.sb("cw", [P, 3, NT, H])
        cm = k.sb("cm", [P, 3, NT, H])
        yt = k.sb("yt", [P, NT, B_OUT])
        pp = k.ps("pp", [P, 8, HALF])
        const_in = k.sem("const_in")
        cleared = k.sem("cleared")
        stored = [k.sem(f"stored{u}") for u in range(2)]
        back = k.sem("back")
        M = [k.steps(f"pe{u}", ["S", "PT", "PV"]) for u in range(2)]
        A = [k.steps(f"act{u}", ["q0", "q1", "e0", "e1", "e2", "e3", "PT"]) for u in range(2)]
        V = [k.steps(f"dve{u}", ["mask", "max", "m", "neg", "rden", "O"]) for u in range(2)]
        CV = k.sem("combine_dve")
        CA = k.sem("combine_act")
        CM = k.sem("combine_pe")
        block = ctx.enter_context(nc.Block())

        def rounds(eng, emit_pair):
            done = 0
            waiting = []
            for group, first, tiles, windows, blk in SEGMENTS:
                if not tiles:
                    waiting.append((done % 2, done // 2, group, first, windows, blk))
                    done += 1
                    if len(waiting) == 2:
                        emit_pair(waiting)
                        waiting = []
                    continue
                with eng.Fori(0, tiles // 2) as i:
                    emit_pair([(u, done // 2 + i, group, first + 2 * i + u, windows, blk) for u in range(2)])
                done += tiles

        def value_tile(group, j, window, windows, blk):
            if group == 0:
                return j - 1 + window if windows == 2 else j
            if group == 1:
                return 8 + j + 4 * (window if windows == 2 else blk)
            return 16 + j

        def keys(group, j, pr, windows, blk):
            kt = QK[:, 6 + group * 2 + pr:7 + group * 2 + pr, :]
            if windows == 1:
                return [moving_tokens(kt, group, j, blk)]
            if group == 0:
                return [moving_tokens(kt, 0, j - 1), moving_tokens(kt, 0, j)]
            return [moving_tokens(kt, 1, j, 0), moving_tokens(kt, 1, j, 1)]

        @block.sync
        def _(sp):
            sp.dma_start(mask_two[:, :], cd["mask_two"]).then_inc(const_in, 16)
            sp.dma_start(mask_pair[:, :], cd["mask_pair"]).then_inc(const_in, 16)

            def pair(items):
                for u, i, group, j, windows, blk in items:
                    rows = scratch[group:group + 1, :, :].rearrange("a t c -> a c t")
                    rows = moving_tokens(rows, group, j, blk)
                    sp.wait_ge(V[u].sem, V[u].after("O", i))
                    sp.dma_start(rows.rearrange("a c b l -> (a b l) c"), ob[u][:, :]).then_inc(stored[u], 16)
            rounds(sp, pair)
            for u in range(2):
                sp.wait_ge(stored[u], 12 * 16)
            for g in range(3):
                sp.dma_start(cb[:, g, :, :], scratch[g].rearrange("(n p) c -> p n c", p=P)).then_inc(back, 16)

        @block.tensor
        def _(pe):
            for u in range(2):
                M[u].start(pe)

            def pair(items):
                for u, i, group, j, windows, blk in items:
                    pe.wait_ge(A[u].sem, A[u].after("q1", i))
                    pe.wait_ge(V[u].sem, V[u].after("O", i - 1))
                    for h in range(H):
                        for wi, kk in enumerate(keys(group, j, h // 2, windows, blk)):
                            out = pp[:, 2 * u + h // 2, (h % 2) * 256 + wi * P:(h % 2) * 256 + (wi + 1) * P]
                            mm = pe.matmul(out, q[u][:, h, :], kk.rearrange("p a r l -> p (a r l)"),
                                           start=True, stop=True)
                    mm.then_inc(M[u].mark("S"), 1)
                for u, i, group, j, windows, blk in items:
                    pe.wait_ge(A[u].sem, A[u].after("e3", i))
                    for h in range(H):
                        for wi in range(windows):
                            mm = pe.transpose(pp[:, 4 + 2 * u + h // 2, (h % 2) * 256 + wi * P:(h % 2) * 256 + (wi + 1) * P],
                                              sm[u][:, h, wi * P:(wi + 1) * P], ident[:, :])
                    mm.then_inc(M[u].mark("PT"), 1)
                for u, i, group, j, windows, blk in items:
                    pe.wait_ge(A[u].sem, A[u].after("PT", i))
                    for h in range(H):
                        for wi in range(windows):
                            v = VS[:, ds(value_tile(group, j, wi, windows, blk), 1), h * HEAD:(h + 1) * HEAD]
                            mm = pe.matmul(pp[:, 2 * u, h * HEAD:(h + 1) * HEAD], pT[u][:, h, wi, :],
                                           v.rearrange("p a c -> p (a c)"), start=wi == 0, stop=wi == windows - 1)
                    mm.then_inc(M[u].mark("PV"), 1)
            rounds(pe, pair)
            pe.wait_ge(CV, 13)
            for n in range(NT):
                for c in range(2):
                    mm = pe.transpose(pp[:, c * 2 + n // 4, (n % 4) * P:(n % 4 + 1) * P],
                                      yt[:, n, c * P:(c + 1) * P], ident[:, :])
            mm.then_inc(CM, 1)

        @block.scalar
        def _(act):
            for u in range(2):
                A[u].start(act)
            act.wait_ge(cleared, 2)

            def pair(items):
                for u, i, group, j, windows, blk in items:
                    act.wait_ge(M[u].sem, M[u].after("S", i - 1))
                    for hf in range(2):
                        rows = slice(hf * HEAD, (hf + 1) * HEAD)
                        src = moving_tokens(QK[rows, group * 2:group * 2 + 2, :], group, j, blk)
                        act.activation(q[u][rows, hf::2, :], src.rearrange("p a r l -> p a (r l)"), ACT.Copy).then_inc(A[u].mark(f"q{hf}"), 1)
                for u, i, group, j, windows, blk in items:
                    act.wait_ge(V[u].sem, V[u].after("neg", i))
                    act.wait_ge(stored[u], 16 * i)
                    for h in range(H):
                        act.activation(sm[u][:, h, 0:windows * P], sm[u][:, h, 0:windows * P], ACT.Exp,
                                       bias=mx[u][:, 1, h:h + 1], scale=HEAD ** -0.5,
                                       accum_out=ob[u][:, B_OUT + H + h:B_OUT + H + h + 1]).then_inc(A[u].mark(f"e{h}"), 1)
                for u, i, group, j, windows, blk in items:
                    act.wait_ge(M[u].sem, M[u].after("PT", i))
                    src = pp[:, 4 + 2 * u:6 + 2 * u, :].rearrange("p b (h n) -> p (b h) n", h=2)[:, :, 0:windows * P]
                    act.activation(pT[u][:, :, 0:windows, :].rearrange("p h w n -> p h (w n)"), src,
                                   ACT.Copy).then_inc(A[u].mark("PT"), 1)
            rounds(act, pair)
            act.wait_ge(CV, 3)
            act.activation(cw[:, :, :, :].rearrange("p g n h -> p (g n h)"),
                           cw[:, :, :, :].rearrange("p g n h -> p (g n h)"), ACT.Exp).then_inc(CA, 1)
            act.wait_ge(CM, 1)
            act.activation(yB[:, :, :].rearrange("p c t -> p (c t)"), pp[:, 0:4, :].rearrange("p b n -> p (b n)"),
                           ACT.Copy).then_inc(CA, 1)

        @block.gpsimd
        def _(pool):
            for u in range(2):
                pool.memset(q[u][:, :, :], 0.0).then_inc(cleared, 1)

        @block.vector
        def _(dve):
            for u in range(2):
                V[u].start(dve)
            dve.wait_ge(const_in, 32)

            def pair(items):
                for u, i, group, j, windows, blk in items:
                    W = windows * P
                    mask = mask_pair if group == 2 else mask_two
                    mask = mask[:, 0:P] if group == 2 else mask[:, (2 - windows) * P:2 * P]
                    dve.wait_ge(M[u].sem, M[u].after("S", i))
                    src = pp[:, 2 * u:2 * u + 2, :].rearrange("p b (h n) -> p (b h) n", h=2)[:, :, 0:W]
                    dve.tensor_tensor(sm[u][:, :, 0:W], src, mask.unsqueeze(1).to_broadcast([P, H, W]),
                                      ALU.add).then_inc(V[u].mark("mask"), 1)
                    dve.wait_ge(V[u].sem, V[u].after("mask", i))
                    dve.tensor_reduce(mx[u][:, 0, :], sm[u][:, :, 0:W], AX.X, ALU.max).then_inc(V[u].mark("max"), 1)
                    dve.wait_ge(V[u].sem, V[u].after("max", i))
                    dve.wait_ge(stored[u], 16 * i)
                    dve.tensor_scalar(ob[u][:, B_OUT:B_OUT + H], mx[u][:, 0, :], HEAD ** -0.5, None,
                                      ALU.mult).then_inc(V[u].mark("m"), 1)
                    dve.tensor_scalar(mx[u][:, 1, :], mx[u][:, 0, :], -HEAD ** -0.5, None,
                                      ALU.mult).then_inc(V[u].mark("neg"), 1)
                for u, i, group, j, windows, blk in items:
                    dve.wait_ge(A[u].sem, A[u].after("e3", i))
                    dve.reciprocal(mx[u][:, 2, :], ob[u][:, B_OUT + H:B_OUT + 2 * H]).then_inc(V[u].mark("rden"), 1)
                    dve.wait_ge(V[u].sem, V[u].after("rden", i))
                    dve.wait_ge(M[u].sem, M[u].after("PV", i))
                    dve.tensor_tensor(ob[u][:, 0:B_OUT].rearrange("p (h c) -> p h c", h=H),
                                      pp[:, 2 * u, 0:B_OUT].rearrange("p (h c) -> p h c", h=H),
                                      mx[u][:, 2, :].unsqueeze(2).to_broadcast([P, H, HEAD]),
                                      ALU.mult).then_inc(V[u].mark("O"), 1)
            rounds(dve, pair)

            step = [0]

            def link(ins):
                step[0] += 1
                ins.then_inc(CV, 1)
                dve.wait_ge(CV, step[0])

            dve.wait_ge(back, 48)
            m = cb[:, :, :, B_OUT:B_OUT + H]
            den = cb[:, :, :, B_OUT + H:OUT_W]
            link(dve.tensor_tensor(cm[:, 0, :, :], m[:, 0], m[:, 1], ALU.max))
            link(dve.tensor_tensor(cm[:, 0, :, :], cm[:, 0, :, :], m[:, 2], ALU.max))
            link(dve.tensor_tensor(cw[:, :, :, :], m, cm[:, 0:1, :, :].to_broadcast([P, 3, NT, H]), ALU.subtract))
            dve.wait_ge(CA, 1)
            link(dve.tensor_tensor(cw[:, :, :, :], cw[:, :, :, :], den, ALU.mult))
            link(dve.tensor_tensor(cm[:, 1, :, :], cw[:, 0, :, :], cw[:, 1, :, :], ALU.add))
            link(dve.tensor_tensor(cm[:, 1, :, :], cm[:, 1, :, :], cw[:, 2, :, :], ALU.add))
            link(dve.reciprocal(cm[:, 2, :, :], cm[:, 1, :, :]))
            link(dve.tensor_tensor(cw[:, :, :, :], cw[:, :, :, :], cm[:, 2:3, :, :].to_broadcast([P, 3, NT, H]), ALU.mult))

            def outputs(g):
                return cb[:, g, :, 0:B_OUT].rearrange("p n (h c) -> p n h c", h=H)

            for g in range(3):
                link(dve.tensor_tensor(outputs(g), outputs(g), cw[:, g, :, :].unsqueeze(3).to_broadcast([P, NT, H, HEAD]),
                                       ALU.mult))
            link(dve.tensor_tensor(yt[:, :, :], cb[:, 0, :, 0:B_OUT], cb[:, 1, :, 0:B_OUT], ALU.add))
            link(dve.tensor_tensor(yt[:, :, :], yt[:, :, :], cb[:, 2, :, 0:B_OUT], ALU.add))


def phase_gmlp(nc, z_u, z_v, ws, bs, ln_w, ln_b, cd, hT, ident, yC):
    with ExitStack() as ctx:
        k = Kit(nc, "gmlp", ctx)
        GROUPS = C_WIDTH // P
        vb = k.sb("vb", [P, NT, C_WIDTH])
        vh = [k.sb(f"vh{u}", [P, C_WIDTH]) for u in range(2)]
        tmp = [k.sb(f"tmp{u}", [P, GROUPS, P]) for u in range(2)]
        wsn = k.sb("wsn", [P, GROUPS, P])
        wsT = k.sb("wsT", [P, GROUPS, P])
        causal = k.sb("causal", [P, P])
        bias = k.sb("bias", [P, GROUPS, P])
        lnw = k.sb("lnw", [P, C_WIDTH])
        lnb = k.sb("lnb", [P, C_WIDTH])
        st = k.sb("st", [P, NT, 2, 6])
        ag = k.sb("ag", [P, NT, 2])
        rs = k.sb("rs", [P, NT])
        pp = k.ps("pp", [P, 8, HALF])
        v_in = [k.sem(f"v_in{t}") for t in range(NT)]
        u_in = [k.sem(f"u_in{t}") for t in range(2)]
        const_in = k.sem("const_in")
        ws_in = k.sem("ws_in")
        ws_mm = k.sem("ws_mm")
        ws_ok = k.sem("ws_ok")
        v_act = k.sem("v_act")
        u_act = k.sem("u_act")
        root = k.sem("root")
        stats = k.sem("stats")
        M = k.steps("pe", ["mix"], 2)
        V = k.steps("dve", ["norm", "w", "b", "bias", "out"], 2)
        block = ctx.enter_context(nc.Block())

        def bank2(b):
            return pp[:, b:b + 2, :].rearrange("p a n -> p (a n)")

        @block.sync
        def _(sp):
            for t in range(NT):
                sp.dma_start(vb[:, t, :], z_v[t * P:(t + 1) * P, :]).then_inc(v_in[t], 16)
            sp.dma_start(wsn[:, :, :], ws.rearrange("g t s -> t g s")).then_inc(ws_in, 16)
            for dst, src in ((causal[:, :], cd["causal"]), (lnw[:, :], ln_w.partition_broadcast(P)),
                             (lnb[:, :], ln_b.partition_broadcast(P)),
                             (bias[:, :, :].rearrange("p g t -> p (g t)"), bs.partition_broadcast(P))):
                sp.dma_start(dst, src).then_inc(const_in, 16)
            for h in range(2):
                sp.dma_start(yC[:, 4 * h:4 * h + 4, :], z_u[h * HALF:(h + 1) * HALF, :].rearrange("(k p) t -> p k t", p=P)).then_inc(u_in[h], 16)

        @block.tensor
        def _(pe):
            M.start(pe)
            pe.wait_ge(ws_in, 16)
            for g in range(GROUPS):
                mm = pe.transpose(bank2(0)[:, g * P:(g + 1) * P], wsn[:, g, :], ident[:, :])
            mm.then_inc(ws_mm, 1)
            pe.wait_ge(ws_ok, 1)
            with pe.Fori(0, NT // 2) as i:
                for u in range(2):
                    n = 2 * i + u
                    pe.wait_ge(V.sem, V.after("b", n))
                    for g in range(GROUPS):
                        mm = pe.matmul(bank2(2 * u)[:, g * P:(g + 1) * P], vh[u][:, g * P:(g + 1) * P], wsT[:, g, :],
                                       start=True, stop=True)
                    mm.then_inc(M.mark("mix"), 1)

        @block.scalar
        def _(act):
            for t in range(NT):
                act.wait_ge(v_in[t], 16)
                act.activation(vb[:, t, :], vb[:, t, :], ACT.Gelu).then_inc(v_act, 1)
            for h in range(2):
                act.wait_ge(u_in[h], 16)
                act.activation(yC[:, 4 * h:4 * h + 4, :], yC[:, 4 * h:4 * h + 4, :], ACT.Gelu).then_inc(u_act, 1)
            act.wait_ge(stats, 25)
            act.activation(rs[:, :], rs[:, :], ACT.Sqrt).then_inc(root, 1)

        @block.vector
        def _(dve):
            V.start(dve)
            for t in range(NT):
                for b in range(2):
                    dve.wait_ge(v_act, t + 1)
                    dve.bn_stats(st[:, t, b, :], vb[:, t, b * HALF:(b + 1) * HALF]).then_inc(stats, 1)
            dve.wait_ge(stats, 16)
            for t in range(NT):
                dve.bn_aggr(ag[:, t, :], st[:, t, :, :]).then_inc(stats, 1)
            dve.wait_ge(stats, 24)
            dve.tensor_scalar(rs[:, :], ag[:, :, 1], LN_EPS, None, ALU.add).then_inc(stats, 1)
            dve.wait_ge(root, 1)
            dve.reciprocal(rs[:, :], rs[:, :]).then_inc(stats, 1)
            dve.wait_ge(const_in, 64)
            dve.wait_ge(stats, 26)
            dve.wait_ge(ws_mm, 1)
            dve.tensor_tensor(wsT[:, :, :], bank2(0).rearrange("p (g n) -> p g n", g=GROUPS),
                              causal[:, :].unsqueeze(1).to_broadcast([P, GROUPS, P]), ALU.mult).then_inc(ws_ok, 1)
            dve.wait_ge(u_act, 2)
            with dve.Fori(0, NT // 2) as i:
                for u in range(2):
                    n = 2 * i + u
                    v = vb[:, ds(n, 1), :].rearrange("p a c -> p (a c)")
                    dve.wait_ge(M.sem, M.after("mix", n - 2))
                    dve.tensor_scalar(v, v, ag[:, ds(n, 1), 0], rs[:, ds(n, 1)], ALU.subtract,
                                      ALU.mult).then_inc(V.mark("norm"), 1)
                    dve.wait_ge(V.sem, V.after("norm", n))
                    dve.tensor_tensor(v, v, lnw[:, :], ALU.mult).then_inc(V.mark("w"), 1)
                    dve.wait_ge(V.sem, V.after("w", n))
                    dve.tensor_tensor(vh[u][:, :], v, lnb[:, :], ALU.add).then_inc(V.mark("b"), 1)
                    dve.wait_ge(M.sem, M.after("mix", n))
                    dve.wait_ge(V.sem, V.after("out", n - 2))
                    dve.tensor_tensor(tmp[u][:, :, :], bank2(2 * u).rearrange("p (g n) -> p g n", g=GROUPS), bias[:, :, :],
                                      ALU.add).then_inc(V.mark("bias"), 1)
                    dve.wait_ge(V.sem, V.after("bias", n))
                    y = yC[:, :, ds(n * P, P)]
                    dve.tensor_tensor(y, tmp[u][:, :, :], y, ALU.mult).then_inc(V.mark("out"), 1)


def phase_merge(nc, z_gates, w_pa, w_pb, w_pc, yA, yB, yC, table, mT):
    with ExitStack() as ctx:
        k = Kit(nc, "merge", ctx)
        zg = [k.sb(f"zg{u}", [P, 3, T]) for u in range(2)]
        wp = [k.sb(f"wp{u}", [P, 2 * KT + 2, P]) for u in range(2)]
        gb = [k.sb(f"gb{u}", [P, 3]) for u in range(2)]
        pr = [k.sb(f"pr{m}", [P, HALF]) for m in range(2)]
        pp = k.ps("pp", [P, 8, HALF])
        w_s = [k.sem(f"w_s{u}") for u in range(2)]
        g_s = [k.sem(f"g_s{u}") for u in range(2)]
        UNITS = [f"{u}{h}{b}" for u in range(2) for h in range(2) for b in range(3)]
        M = k.steps("pe", ["b" + x for x in UNITS])
        A = k.steps("act", [f"{u}{b}" for u in range(2) for b in range(3)])
        V = k.steps("dve", [n for x in UNITS for n in
                            ((["bias" + x[0]] if x[1] == "0" else []) + ["p" + x] if x[2] == "0" else ["p" + x, "s" + x])])
        block = ctx.enter_context(nc.Block())
        gate_b = ROWS["gate_b"][0]

        def unit(u, h, b, back=0):
            n = UNITS.index(f"{u}{h}{b}") - back
            return UNITS[n % 12], n // 12

        @block.sync
        def _(sp):
            with sp.Fori(0, KT // 2) as i:
                for u in range(2):
                    col = (2 * i + u) * P
                    sp.wait_ge(V.sem, V.after(f"s{u}12", i - 1))
                    sp.dma_start(zg[u][:, :, :], z_gates[0:3 * D, :].rearrange("(b k p) t -> p b k t", b=3, p=P)[:, :, ds(2 * i + u, 1), :]
                                 .rearrange("p b k t -> p (b k) t")).then_inc(g_s[u], 16)
                    sp.dma_start(wp[u][:, 0:KT, :], weight_columns(w_pa, col, P)).then_inc(w_s[u], 16)
                    sp.dma_start(wp[u][:, KT:2 * KT, :], weight_columns(w_pc, col, P)).then_inc(w_s[u], 16)
                    sp.dma_start(wp[u][:, 2 * KT:, :], weight_columns(w_pb, col, P)).then_inc(w_s[u], 16)

        @block.tensor
        def _(pe):
            M.start(pe)
            with pe.Fori(0, KT // 2) as i:
                for u in range(2):
                    pe.wait_ge(w_s[u], 48 * i + 48)
                    for h in range(2):
                        for b in range(3):
                            bank = (u * 6 + h * 3 + b) % 4
                            x, r = unit(u, h, b, 4)
                            pe.wait_ge(V.sem, V.after("p" + x, i + r))
                            cols = slice(h * HALF, (h + 1) * HALF)
                            y, at, n = ((yA, 0, KT), (yB, 2 * KT, 2), (yC, KT, KT))[b]
                            for kt in range(n):
                                mm = pe.matmul(pp[:, bank, :], wp[u][:, at + kt, :], y[:, kt, cols], start=kt == 0, stop=kt == n - 1)
                            mm.then_inc(M.mark(f"b{u}{h}{b}"), 1)

        @block.scalar
        def _(act):
            A.start(act)
            with act.Fori(0, KT // 2) as i:
                for u in range(2):
                    act.wait_ge(g_s[u], 16 * i + 16)
                    act.wait_ge(V.sem, V.after(f"bias{u}", i))
                    for b in range(3):
                        act.activation(zg[u][:, b, :], zg[u][:, b, :], ACT.Sigmoid, bias=gb[u][:, b:b + 1]).then_inc(A.mark(f"{u}{b}"), 1)

        @block.vector
        def _(dve):
            V.start(dve)
            with dve.Fori(0, KT // 2) as i:
                for u in range(2):
                    dve.wait_ge(A.sem, A.after(f"{u}2", i - 1))
                    biases = table[:, gate_b:gate_b + 3 * KT].rearrange("p (b t) -> p b t", b=3)[:, :, ds(2 * i + u, 1)]
                    dve.tensor_copy(gb[u][:, :].unsqueeze(2), biases).then_inc(V.mark(f"bias{u}"), 1)
                    for h in range(2):
                        dst = mT[:, ds(2 * i + u, 1), h * HALF:(h + 1) * HALF].rearrange("p a n -> p (a n)")
                        for b in range(3):
                            m = (u * 6 + h * 3 + b) % 4
                            sg = zg[u][:, b, h * HALF:(h + 1) * HALF]
                            dve.wait_ge(A.sem, A.after(f"{u}{b}", i))
                            dve.wait_ge(M.sem, M.after(f"b{u}{h}{b}", i))
                            if b == 0:
                                dve.tensor_tensor(dst, pp[:, m, :], sg, ALU.mult).then_inc(V.mark(f"p{u}{h}0"), 1)
                                continue
                            x, r = unit(u, h, b, 3)
                            dve.wait_ge(V.sem, V.after("s" + x if x[2] != "0" else "p" + x, i + r))
                            dve.tensor_tensor(pr[b - 1][:, :], pp[:, m, :], sg, ALU.mult).then_inc(V.mark(f"p{u}{h}{b}"), 1)
                            dve.wait_ge(V.sem, V.after(f"p{u}{h}{b}", i))
                            dve.tensor_tensor(dst, dst, pr[b - 1][:, :], ALU.add).then_inc(V.mark(f"s{u}{h}{b}"), 1)


def phase_out(nc, x, w_out, wr_g, wr_e, rb_g, rb_e, mT, table, ident, x2_d, h2_d, LG):
    with ExitStack() as ctx:
        k = Kit(nc, "out", ctx)
        wo = k.sb("wo", [P, KT, D])
        wr = k.sb("wr", [P, KT, 40])
        rb = k.sb("rb", [P, 40])
        xt = [k.sb(f"xt{u}", [P, D]) for u in range(2)]
        h2 = [k.sb(f"h2{u}", [P, D]) for u in range(2)]
        hb = [k.sb(f"hb{u}", [P, KT, P]) for u in range(2)]
        junk = k.sb("junk", [P, D])
        st = [k.sb(f"st{u}", [P, 4]) for u in range(2)]
        pp = k.ps("pp", [P, 8, HALF])
        x_in = [k.sem(f"x_in{u}") for u in range(2)]
        wo_in = k.sem("wo_in")
        wr_in = k.sem("wr_in")
        cleared = k.sem("cleared")
        x2_out = [k.sem(f"x2_out{u}") for u in range(2)]
        h2_out = [k.sem(f"h2_out{u}") for u in range(2)]
        proj = k.sem("proj")
        turned = k.sem("turned")
        logits = k.sem("logits")
        A = k.steps("act", ["squares", "root"], 2)
        V = k.steps("dve", ["x2", "mean", "rstd", "h2", "hb", "logits"], 2)
        block = ctx.enter_context(nc.Block())

        def bank2(b):
            return pp[:, b:b + 2, :].rearrange("p a n -> p (a n)")

        @block.sync
        def _(sp):
            sp.dma_start(wo[:, :, :], w_out.rearrange("(k p) n -> p k n", p=P)).then_inc(wo_in, 16)
            sp.wait_ge(cleared, 2)
            sp.dma_start(wr[:, :, 0:4], wr_g.rearrange("(k p) n -> p k n", p=P)).then_inc(wr_in, 16)
            sp.dma_start(wr[:, :, 8:40], wr_e.rearrange("(k p) n -> p k n", p=P)).then_inc(wr_in, 16)
            sp.dma_start(rb[:, 0:4], rb_g.partition_broadcast(P)).then_inc(wr_in, 16)
            sp.dma_start(rb[:, 8:40], rb_e.partition_broadcast(P)).then_inc(wr_in, 16)
            for t in range(NT + 1):
                if t < NT:
                    u = t % 2
                    if t >= 2:
                        sp.wait_ge(x2_out[u], 16 * (t // 2))
                        sp.wait_ge(V.sem, V.after("h2", t - 2))
                        sp.wait_ge(A.sem, A.after("squares", t - 2))
                    sp.dma_start(xt[u][:, :], x[t * P:(t + 1) * P, :]).then_inc(x_in[u], 16)
                if t >= 1:
                    u = (t - 1) % 2
                    rows = slice((t - 1) * P, t * P)
                    sp.wait_ge(V.sem, V.after("x2", t - 1))
                    sp.dma_start(x2_d[rows, :], xt[u][:, :]).then_inc(x2_out[u], 16)
                    sp.wait_ge(V.sem, V.after("h2", t - 1))
                    sp.dma_start(h2_d[rows, :], h2[u][:, :]).then_inc(h2_out[u], 16)
            for u in range(2):
                sp.wait_ge(x2_out[u], 16 * NT // 2)
                sp.wait_ge(h2_out[u], 16 * NT // 2)

        @block.gpsimd
        def _(pool):
            pool.memset(wr[:, :, :], 0.0).then_inc(cleared, 1)
            pool.memset(rb[:, :], NEG).then_inc(cleared, 1)

        @block.tensor
        def _(pe):
            pe.wait_ge(wo_in, 16)
            for t in range(NT + 1):
                if t < NT:
                    pe.wait_ge(V.sem, V.after("x2", t - 2))
                    for h in range(2):
                        for kt in range(KT):
                            mm = pe.matmul(pp[:, 2 * (t % 2) + h, :], mT[:, kt, t * P:(t + 1) * P],
                                           wo[:, kt, h * HALF:(h + 1) * HALF], start=kt == 0, stop=kt == KT - 1)
                    mm.then_inc(proj, 1)
                if t >= 1:
                    n, u = t - 1, (t - 1) % 2
                    if n == 0:
                        pe.wait_ge(wr_in, 64)
                    pe.wait_ge(V.sem, V.after("h2", n))
                    for kt in range(KT):
                        mm = pe.transpose(bank2(4)[:, kt * P:(kt + 1) * P], h2[u][:, kt * P:(kt + 1) * P], ident[:, :])
                    mm.then_inc(turned, 1)
                    pe.wait_ge(V.sem, V.after("hb", n))
                    for kt in range(KT):
                        mm = pe.matmul(pp[:, 6 + u, 0:40], hb[u][:, kt, :], wr[:, kt, :], start=kt == 0, stop=kt == KT - 1)
                    mm.then_inc(logits, 1)

        @block.scalar
        def _(act):
            A.start(act)
            for t in range(NT):
                u = t % 2
                act.wait_ge(V.sem, V.after("x2", t))
                act.wait_ge(V.sem, V.after("h2", t - 2))
                act.wait_ge(A.sem, A.after("squares", t - 1))
                act.activation(junk[:, :], xt[u][:, :], ACT.Square, accum_out=st[u][:, 0:1]).then_inc(A.mark("squares"), 1)
                act.wait_ge(V.sem, V.after("mean", t))
                act.activation(st[u][:, 2:3], st[u][:, 1:2], ACT.Sqrt).then_inc(A.mark("root"), 1)

        @block.vector
        def _(dve):
            V.start(dve)
            for t in range(NT):
                u = t % 2
                dve.wait_ge(x_in[u], 16 * (t // 2) + 16)
                dve.wait_ge(proj, t + 1)
                dve.tensor_tensor(xt[u][:, :], bank2(2 * u), xt[u][:, :], ALU.add).then_inc(V.mark("x2"), 1)
                dve.wait_ge(A.sem, A.after("squares", t))
                dve.tensor_scalar(st[u][:, 1:2], st[u][:, 0:1], 1.0 / D, RMS_EPS, ALU.mult, ALU.add).then_inc(V.mark("mean"), 1)
                dve.wait_ge(A.sem, A.after("root", t))
                dve.reciprocal(st[u][:, 3:4], st[u][:, 2:3]).then_inc(V.mark("rstd"), 1)
                dve.wait_ge(V.sem, V.after("rstd", t))
                if t >= 2:
                    dve.wait_ge(h2_out[u], 16 * (t // 2))
                    dve.wait_ge(turned, t - 1)
                dve.tensor_scalar(h2[u][:, :], xt[u][:, :], st[u][:, 3:4], None, ALU.mult).then_inc(V.mark("h2"), 1)
                dve.wait_ge(turned, t + 1)
                nf = table[:, ROWS["norm_ffn"][0]:ROWS["norm_ffn"][0] + KT].unsqueeze(2).to_broadcast([P, KT, P])
                if t >= 2:
                    dve.wait_ge(logits, t - 1)
                dve.tensor_tensor(hb[u][:, :, :], bank2(4).rearrange("p (k n) -> p k n", k=KT), nf, ALU.mult).then_inc(V.mark("hb"), 1)
                dve.wait_ge(logits, t + 1)
                dve.tensor_tensor(LG[:, t, :], pp[:, 6 + u, 0:40], rb[:, :], ALU.add).then_inc(V.mark("logits"), 1)


def phase_route(nc, cd, LG, ident, slot_u, wts, extra_i, tok_d, tok_u):
    with ExitStack() as ctx:
        k = Kit(nc, "route", ctx)
        BLOCKS = N_EXPERTS + MAX_EXTRA
        before = k.sb("before", [P, P])
        ones = k.sb("ones", [P, P])
        thr = k.sb("thr", [P, 7])
        eids = k.sb("eids", [P, N_EXPERTS])
        xids = k.sb("xids", [P, MAX_EXTRA])
        tids = k.sb("tids", [P, NT])
        zero = k.sb("zero", [BLOCKS, P])
        g8 = k.sb("g8", [P, NT, 8])
        gi = k.sb("gi", [P, NT, 8], U32)
        e8 = k.sb("e8", [P, NT, 8])
        ei = k.sb("ei", [P, NT, 8], U32)
        gf = k.sb("gf", [P, NT])
        ef = k.sb("ef", [P, NT, 2])
        goh = k.sb("goh", [P, NT, N_GROUPS])
        em = k.sb("em", [P, NT, N_EXPERTS])
        ex = k.sb("ex", [P, NT, N_GROUPS + 1])
        sums = k.sb("sums", [P, NT, 3])
        O = k.sb("O", [P, 3, NT, N_EXPERTS])
        cnt = k.sb("cnt", [P, N_EXPERTS, 7])
        over = k.sb("over", [P, 6, N_EXPERTS])
        sl = k.sb("sl", [P, NT, N_EXPERTS])
        ov = k.sb("ov", [P, NT, N_EXPERTS])
        slot = k.sb("slot", [P, 2, NT])
        xe = k.sb("xe", [P, MAX_EXTRA, N_EXPERTS])
        xe2 = k.sb("xe2", [P, MAX_EXTRA, N_EXPERTS])
        xf = k.sb("xf", [P, MAX_EXTRA + 1])
        tok = k.sb("tok", [BLOCKS, P])
        pos = k.ps("pos", [P, NT, N_EXPERTS])
        tot = k.ps("tot", [P, HALF])
        tt = k.ps("tt", [P, HALF])
        const_in = k.sem("const_in")
        zeroed = k.sem("zeroed")
        scattered = k.sem("scattered")
        tok_in = k.sem("tok_in")
        C = k.sem("dve")
        exps = k.sem("exps")
        counted = k.sem("counted")
        turned = k.sem("turned")
        cleared = k.sem("cleared")
        marks = {}
        block = ctx.enter_context(nc.Block())

        def wide(ap, shape):
            return ap.to_broadcast(shape)

        @block.vector
        def _(dve):
            step = [0]

            def link(ins, name=None):
                step[0] += 1
                marks[name] = step[0]
                ins.then_inc(C, 1)
                dve.wait_ge(C, step[0])

            dve.wait_ge(const_in, 96)
            for t in range(NT):
                link(dve.max(g8[:, t, :], LG[:, t, 0:8]))
                link(dve.max_index(gi[:, t, :], g8[:, t, :], LG[:, t, 0:8]))
            link(dve.tensor_copy(gf[:, :], gi[:, :, 0]))
            link(dve.tensor_tensor(goh[:, :, :], wide(eids[:, 0:4].unsqueeze(1), [P, NT, 4]),
                                   wide(gf[:, :].unsqueeze(2), [P, NT, 4]), ALU.is_equal))
            link(dve.tensor_scalar(goh[:, :, :], goh[:, :, :], -1.0, -NEG, ALU.add, ALU.mult))
            link(dve.tensor_tensor(em[:, :, :].rearrange("p t (g e) -> p t g e", g=4),
                                   LG[:, :, 8:40].rearrange("p t (g e) -> p t g e", g=4),
                                   wide(goh[:, :, :].unsqueeze(3), [P, NT, 4, 8]), ALU.add))
            for t in range(NT):
                link(dve.max(e8[:, t, :], em[:, t, :]))
                link(dve.max_index(ei[:, t, :], e8[:, t, :], em[:, t, :]))
            link(dve.tensor_tensor(ex[:, :, 0:4], LG[:, :, 0:4], wide(g8[:, :, 0:1], [P, NT, 4]), ALU.subtract))
            link(dve.tensor_tensor(ex[:, :, 4:5], e8[:, :, 1:2], e8[:, :, 0:1], ALU.subtract), "exponents")
            link(dve.tensor_copy(ef[:, :, :], ei[:, :, 0:2]))
            for j in range(2):
                link(dve.tensor_tensor(O[:, j, :, :], wide(eids[:, :].unsqueeze(1), [P, NT, N_EXPERTS]),
                                       wide(ef[:, :, j:j + 1], [P, NT, N_EXPERTS]), ALU.is_equal))
            link(dve.tensor_tensor(O[:, 2, :, :], O[:, 0, :, :], O[:, 1, :, :], ALU.add), "onehots")
            dve.wait_ge(exps, 1)
            link(dve.tensor_reduce(sums[:, :, 0], ex[:, :, 0:4], AX.X, ALU.add))
            link(dve.tensor_scalar(sums[:, :, 1], ex[:, :, 4], 1.0, None, ALU.add))
            link(dve.tensor_tensor(sums[:, :, 2], sums[:, :, 0], sums[:, :, 1], ALU.mult))
            link(dve.reciprocal(wts[:, 0, :], sums[:, :, 2]))
            link(dve.tensor_tensor(wts[:, 1, :], wts[:, 0, :], ex[:, :, 4], ALU.mult))
            dve.wait_ge(counted, 1)
            link(dve.tensor_tensor(cnt[:, :, :], wide(tot[:, 0:N_EXPERTS].unsqueeze(2), [P, N_EXPERTS, 7]),
                                   wide(thr[:, :].unsqueeze(1), [P, N_EXPERTS, 7]), ALU.is_gt))
            link(dve.tensor_reduce(over[:, 0, :], cnt[:, :, :], AX.X, ALU.add))
            link(dve.memset(over[:, 5, :], 1.0))
            link(dve.tensor_tensor_scan(over[:, 1, :], over[:, 5, :], over[:, 0, :], 0.0, ALU.mult, ALU.add))
            link(dve.tensor_tensor(over[:, 2, :], over[:, 1, :], over[:, 0, :], ALU.subtract))
            link(dve.tensor_scalar(over[:, 4, :], eids[:, :], float(SLOTS), None, ALU.mult))
            link(dve.tensor_scalar(over[:, 3, :], over[:, 2, :], float(SLOTS), float((N_EXPERTS - 1) * SLOTS), ALU.mult, ALU.add))
            link(dve.tensor_tensor(over[:, 3, :], over[:, 3, :], over[:, 4, :], ALU.subtract))
            link(dve.tensor_scalar(ov[:, :, :], pos[:, :, :], float(SLOTS), None, ALU.is_ge))
            link(dve.tensor_tensor(ov[:, :, :], ov[:, :, :], wide(over[:, 3:4, :], [P, NT, N_EXPERTS]), ALU.mult))
            link(dve.tensor_tensor(sl[:, :, :], pos[:, :, :], wide(over[:, 4:5, :], [P, NT, N_EXPERTS]), ALU.add))
            link(dve.tensor_tensor(sl[:, :, :], sl[:, :, :], ov[:, :, :], ALU.add))
            for j in range(2):
                link(dve.tensor_tensor(O[:, j, :, :], O[:, j, :, :], sl[:, :, :], ALU.mult))
                link(dve.tensor_reduce(slot[:, j, :], O[:, j, :, :], AX.X, ALU.add))
            link(dve.tensor_copy(slot_u[:, :, :], slot[:, :, :]), "slots")
            shape = [P, MAX_EXTRA, N_EXPERTS]
            link(dve.tensor_tensor(xe[:, :, :], wide(xids[:, :].unsqueeze(2), shape), wide(over[:, 2:3, :], shape), ALU.is_ge))
            link(dve.tensor_tensor(xe2[:, :, :], wide(xids[:, :].unsqueeze(2), shape), wide(over[:, 1:2, :], shape), ALU.is_lt))
            link(dve.tensor_tensor(xe[:, :, :], xe[:, :, :], xe2[:, :, :], ALU.mult))
            link(dve.tensor_tensor(xe[:, :, :], xe[:, :, :], wide(eids[:, :].unsqueeze(1), shape), ALU.mult))
            link(dve.tensor_reduce(xf[:, 0:MAX_EXTRA], xe[:, :, :], AX.X, ALU.add))
            link(dve.tensor_copy(xf[:, MAX_EXTRA:], over[:, 1, N_EXPERTS - 1:]))
            link(dve.tensor_copy(extra_i[:, :], xf[:, :]))
            dve.wait_ge(turned, 1)
            link(dve.tensor_copy(tok_u[:, :], tt[:, 0:BLOCKS]))

        @block.sync
        def _(sp):
            for dst, src in ((before, "before"), (ones, "ones"), (thr, "thresholds"), (eids, "expert_ids"),
                             (xids, "extra_ids"), (tids, "token_ids")):
                sp.dma_start(dst[:, :], cd[src]).then_inc(const_in, 16)
            sp.wait_ge(cleared, 1)
            sp.dma_start(tok_d.rearrange("(b s) o -> b (s o)", s=SLOTS), zero[:, :]).then_inc(zeroed, 16)
            sp.wait_ge(scattered, 16 * 2 * NT)
            sp.dma_start(tok[:, :], tok_d.rearrange("(b s) o -> b (s o)", s=SLOTS)).then_inc(tok_in, 16)

        @block.scalar
        def _(act):
            act.wait_ge(C, marks["exponents"])
            act.activation(ex[:, :, :].rearrange("p t g -> p (t g)"), ex[:, :, :].rearrange("p t g -> p (t g)"),
                           ACT.Exp).then_inc(exps, 1)

        @block.tensor
        def _(pe):
            pe.wait_ge(C, marks["onehots"])
            pe.wait_ge(const_in, 96)
            for t in range(NT):
                for i in range(t):
                    pe.matmul(pos[:, t, :], ones[:, :], O[:, 2, i, :], start=i == 0, stop=False)
                pe.matmul(pos[:, t, :], before[:, :], O[:, 2, t, :], start=t == 0, stop=True)
            for t in range(NT):
                mm = pe.matmul(tot[:, 0:N_EXPERTS], ones[:, :], O[:, 2, t, :], start=t == 0, stop=t == NT - 1)
            mm.then_inc(counted, 1)
            pe.wait_ge(tok_in, 16)
            pe.transpose(tt[:, 0:BLOCKS], tok[:, :], ident[0:BLOCKS, 0:BLOCKS]).then_inc(turned, 1)

        @block.gpsimd
        def _(pool):
            pool.memset(zero[:, :], 0.0).then_inc(cleared, 1)
            pool.wait_ge(const_in, 96)
            pool.wait_ge(zeroed, 16)
            pool.wait_ge(C, marks["slots"])
            for t in range(NT):
                for j in range(2):
                    pool.indirect_dma_start(tok_d, bass.IndirectOffsetOnAxis(ap=slot_u[:, j, t:t + 1], axis=0),
                                            tids[:, t:t + 1], None).then_inc(scattered, 16)


def phase_experts(nc, w1_d, w3_d, w2_d, h2_d, y_d, table, ident, tok_u, extra_i):
    for tag, extra in (("own", False), ("extra", True)):
        with ExitStack() as ctx:
            k = Kit(nc, tag, ctx)
            NB = 1 if extra else 2
            w1 = [k.sb(f"w1{u}", [P, KT, FF]) for u in range(NB)]
            w3 = [k.sb(f"w3{u}", [P, KT, FF]) for u in range(NB)]
            w2 = [k.sb(f"w2{u}", [P, FF // P, D]) for u in range(NB)]
            ix = [k.sb(f"ix{u}", [P, 1], U32) for u in range(NB)]
            xg = [k.sb(f"xg{u}", [P, D]) for u in range(NB)]
            xT = [k.sb(f"xT{u}", [P, KT, P]) for u in range(NB)]
            act_h = [k.sb(f"act_h{u}", [P, FF]) for u in range(NB)]
            hid = [k.sb(f"hid{u}", [P, FF]) for u in range(NB)]
            hidT = [k.sb(f"hidT{u}", [P, FF // P, P]) for u in range(NB)]
            yo = [k.sb(f"yo{u}", [P, D]) for u in range(NB)]
            pp = k.ps("pp", [P, 8, HALF])
            w_s = [k.sem(f"w_s{u}") for u in range(NB)]
            w2_s = [k.sem(f"w2_s{u}") for u in range(NB)]
            x_s = [k.sem(f"x_s{u}") for u in range(NB)]
            y_s = [k.sem(f"y_s{u}") for u in range(NB)]
            M = k.steps("pe", ["turn", "w1", "w3", "turn_h", "w2"], 2)
            A = k.steps("act", ["silu", "hidT", "y"], 2)
            V = k.steps("dve", ["xT", "hid"], 2)
            Q = k.steps("pool", ["ix"], 2)
            go = k.sem("go")
            block = ctx.enter_context(nc.Block())
            blocks = MAX_EXTRA if extra else N_EXPERTS

            def bank2(b):
                return pp[:, b:b + 2, :].rearrange("p a n -> p (a n)")

            def each(eng, body, end=None):
                if not extra:
                    with eng.Fori(0, blocks // NB) as i:
                        for u in range(NB):
                            body(u, i, NB * i + u)
                    if end:
                        end(blocks // NB)
                    return
                some = eng.value_load(extra_i[0:1, MAX_EXTRA:MAX_EXTRA + 1], min_val=0, max_val=MAX_EXTRA)
                with eng.Fori(0, blocks) as i:
                    with eng.If(i < some):
                        body(0, i, i)
                if end:
                    end(some)

            @block.sync
            def _(sp):
                def body(u, i, n):
                    e = n
                    if extra:
                        e = sp.value_load(extra_i[0:1, ds(n, 1)], min_val=0, max_val=N_EXPERTS - 1)
                    sp.wait_ge(M.sem, M.after("w3", n - NB))
                    for w, w_d in ((w1, w1_d), (w3, w3_d)):
                        sp.dma_start(w[u][:, :, :], w_d[ds(e, 1), :, :].rearrange("a (k p) n -> p (a k) n", p=P)).then_inc(w_s[u], 16)
                    sp.wait_ge(M.sem, M.after("w2", n - NB))
                    sp.dma_start(w2[u][:, :, :], w2_d[ds(e, 1), :, :].rearrange("a (k p) n -> p (a k) n", p=P)).then_inc(w2_s[u], 16)
                each(sp, body)

            @block.gpsimd
            def _(pool):
                Q.start(pool)

                def body(u, i, n):
                    b = n + (N_EXPERTS if extra else 0)
                    pool.wait_ge(M.sem, M.after("turn", n - NB))
                    pool.tensor_copy(ix[u][:, :], tok_u[:, ds(b, 1)]).then_inc(Q.mark("ix"), 1)
                    pool.wait_ge(Q.sem, Q.after("ix", n))
                    pool.sem_inc(go, 1)
                    pool.indirect_dma_start(xg[u][:, :], None, h2_d, bass.IndirectOffsetOnAxis(ap=ix[u][:, :], axis=0)).then_inc(x_s[u], 16)

                def end(rounds):
                    for u in range(NB):
                        pool.wait_ge(y_s[u], 16 * rounds + 16)
                each(pool, body, end)

            @block.tensor
            def _(pe):
                M.start(pe)

                def body(u, i, n):
                    pe.wait_ge(x_s[u], 16 * i + 16)
                    pe.wait_ge(V.sem, V.after("xT", n - 1))
                    for kt in range(KT):
                        mm = pe.transpose(bank2(0)[:, kt * P:(kt + 1) * P], xg[u][:, kt * P:(kt + 1) * P], ident[:, :])
                    mm.then_inc(M.mark("turn"), 1)
                    pe.wait_ge(w_s[u], 32 * i + 32)
                    pe.wait_ge(V.sem, V.after("xT", n))
                    for name, w, bank in (("w1", w1, 2), ("w3", w3, 3)):
                        for kt in range(KT):
                            mm = pe.matmul(pp[:, bank, :], xT[u][:, kt, :], w[u][:, kt, :], start=kt == 0, stop=kt == KT - 1)
                        mm.then_inc(M.mark(name), 1)
                    pe.wait_ge(V.sem, V.after("hid", n))
                    pe.wait_ge(A.sem, A.after("hidT", n - 1))
                    for j in range(FF // P):
                        mm = pe.transpose(pp[:, 4, j * P:(j + 1) * P], hid[u][:, j * P:(j + 1) * P], ident[:, :])
                    mm.then_inc(M.mark("turn_h"), 1)
                    pe.wait_ge(w2_s[u], 16 * i + 16)
                    pe.wait_ge(A.sem, A.after("y", n - 1))
                    pe.wait_ge(A.sem, A.after("hidT", n))
                    for h in range(2):
                        for j in range(FF // P):
                            mm = pe.matmul(pp[:, 6 + h, :], hidT[u][:, j, :], w2[u][:, j, h * HALF:(h + 1) * HALF],
                                           start=j == 0, stop=j == FF // P - 1)
                    mm.then_inc(M.mark("w2"), 1)
                each(pe, body)

            @block.scalar
            def _(act):
                A.start(act)
                for u in range(NB):
                    act.sem_inc(y_s[u], 16)

                def body(u, i, n):
                    act.wait_ge(M.sem, M.after("w1", n))
                    act.wait_ge(V.sem, V.after("hid", n - NB))
                    act.activation(act_h[u][:, :], pp[:, 2, :], ACT.Silu).then_inc(A.mark("silu"), 1)
                    act.wait_ge(M.sem, M.after("turn_h", n))
                    act.activation(hidT[u][:, :, :].rearrange("p j n -> p (j n)"), pp[:, 4, :], ACT.Copy).then_inc(A.mark("hidT"), 1)
                    act.wait_ge(M.sem, M.after("w2", n))
                    act.wait_ge(y_s[u], 16 * i + 16)
                    act.activation(yo[u][:, :], bank2(6), ACT.Copy).then_inc(A.mark("y"), 1)
                    act.wait_ge(A.sem, A.after("y", n))
                    b = n + (N_EXPERTS if extra else 0)
                    act.dma_start(y_d[ds(b * SLOTS, SLOTS), :], yo[u][:, :]).then_inc(y_s[u], 16)
                each(act, body)

            @block.vector
            def _(dve):
                V.start(dve)
                nf = table[:, ROWS["norm_ffn"][0]:ROWS["norm_ffn"][0] + KT].unsqueeze(2).to_broadcast([P, KT, P])

                def body(u, i, n):
                    dve.wait_ge(M.sem, M.after("turn", n))
                    dve.wait_ge(M.sem, M.after("w3", n - NB))
                    dve.tensor_tensor(xT[u][:, :, :], bank2(0).rearrange("p (k n) -> p k n", k=KT), nf, ALU.mult).then_inc(V.mark("xT"), 1)
                    dve.wait_ge(M.sem, M.after("w3", n))
                    dve.wait_ge(A.sem, A.after("silu", n))
                    dve.tensor_tensor(hid[u][:, :], pp[:, 3, :], act_h[u][:, :], ALU.mult).then_inc(V.mark("hid"), 1)
                each(dve, body)


def phase_final(nc, x2_d, y_d, norm_final, slot_u, wts, out):
    with ExitStack() as ctx:
        k = Kit(nc, "final", ctx)
        nf = k.sb("nf", [P, D])
        junk = k.sb("junk", [P, D])
        x2 = [k.sb(f"x2{u}", [P, D]) for u in range(2)]
        y1 = [k.sb(f"y1{u}", [P, D]) for u in range(2)]
        y2 = [k.sb(f"y2{u}", [P, D]) for u in range(2)]
        st = [k.sb(f"st{u}", [P, 4]) for u in range(2)]
        nf_in = k.sem("nf_in")
        x_in = [k.sem(f"x_in{u}") for u in range(2)]
        y_in = [k.sem(f"y_in{u}") for u in range(2)]
        done = [k.sem(f"done{u}") for u in range(2)]
        A = k.steps("act", ["squares", "root"], 2)
        V = k.steps("dve", ["add1", "add2", "mean", "rstd", "out"], 2)
        block = ctx.enter_context(nc.Block())

        @block.sync
        def _(sp):
            sp.dma_start(nf[:, :], norm_final.partition_broadcast(P)).then_inc(nf_in, 16)
            for t in range(NT + 1):
                if t < NT:
                    u = t % 2
                    if t >= 2:
                        sp.wait_ge(done[u], 16 * (t // 2))
                    sp.dma_start(x2[u][:, :], x2_d[t * P:(t + 1) * P, :]).then_inc(x_in[u], 16)
                if t >= 1:
                    sp.wait_ge(V.sem, V.after("out", t - 1))
                    sp.dma_start(out[(t - 1) * P:t * P, :], x2[(t - 1) % 2][:, :]).then_inc(done[(t - 1) % 2], 16)
            for u in range(2):
                sp.wait_ge(done[u], 16 * NT // 2)

        @block.gpsimd
        def _(pool):
            for t in range(NT):
                u = t % 2
                pool.wait_ge(V.sem, V.after("add2", t - 2))
                for j, y in enumerate((y1, y2)):
                    pool.indirect_dma_start(y[u][:, :], None, y_d,
                                            bass.IndirectOffsetOnAxis(ap=slot_u[:, j, t:t + 1], axis=0)).then_inc(y_in[u], 16)

        @block.scalar
        def _(act):
            A.start(act)
            for t in range(NT):
                u = t % 2
                act.wait_ge(V.sem, V.after("add2", t))
                act.wait_ge(A.sem, A.after("squares", t - 1))
                act.activation(junk[:, :], x2[u][:, :], ACT.Square, accum_out=st[u][:, 0:1]).then_inc(A.mark("squares"), 1)
                act.wait_ge(V.sem, V.after("mean", t))
                act.activation(st[u][:, 2:3], st[u][:, 1:2], ACT.Sqrt).then_inc(A.mark("root"), 1)

        @block.vector
        def _(dve):
            V.start(dve)
            dve.wait_ge(nf_in, 16)
            for t in range(NT):
                u = t % 2
                dve.wait_ge(x_in[u], 16 * (t // 2) + 16)
                dve.wait_ge(y_in[u], 32 * (t // 2) + 32)
                for j, y in enumerate((y1, y2)):
                    dve.scalar_tensor_tensor(out=x2[u][:, :], in0=y[u][:, :], scalar=wts[:, j, t:t + 1], in1=x2[u][:, :],
                                             op0=ALU.mult, op1=ALU.add).then_inc(V.mark(f"add{j + 1}"), 1)
                    dve.wait_ge(V.sem, V.after(f"add{j + 1}", t))
                dve.wait_ge(A.sem, A.after("squares", t))
                dve.tensor_scalar(st[u][:, 1:2], st[u][:, 0:1], 1.0 / D, RMS_EPS, ALU.mult, ALU.add).then_inc(V.mark("mean"), 1)
                dve.wait_ge(A.sem, A.after("root", t))
                dve.reciprocal(st[u][:, 3:4], st[u][:, 2:3]).then_inc(V.mark("rstd"), 1)
                dve.wait_ge(V.sem, V.after("rstd", t))
                dve.scalar_tensor_tensor(out=x2[u][:, :], in0=x2[u][:, :], scalar=st[u][:, 3:4], in1=nf[:, :],
                                         op0=ALU.mult, op1=ALU.mult).then_inc(V.mark("out"), 1)


def program(nc, d, c, out):
    with ExitStack() as ctx:
        k = Kit(nc, "main", ctx)
        ident = k.sb("ident", [P, P])
        table = k.sb("table", [P, N_ROWS])
        LG = k.sb("LG", [P, NT, 40])
        slot_u = k.sb("slot_u", [P, 2, NT], U32)
        wts = k.sb("wts", [P, 2, NT])
        extra_i = k.sb("extra_i", [P, MAX_EXTRA + 1], I32)
        tok_u = k.sb("tok_u", [P, N_EXPERTS + MAX_EXTRA], U32)
        with ExitStack() as mixers:
            k = Kit(nc, "mix", mixers)
            hT = k.sb("hT", [P, KT, T])
            phase_norm(nc, d["x"], [(ROWS[n][0], d[n]) for n in ROWS], c["ident"], hT, table, ident)
            phase_rwkv(nc, d["w_in"], d["w_decay2"], d["a2"], d["g2"], c, hT, table, ident, d["ya"],
                       d["z_channel"], d["z_token"])
            yA = k.sb("yA", [P, PAIRS, T])
            yB = k.sb("yB", [P, B_OUT // P, T])
            with ExitStack() as attention:
                ka = Kit(nc, "att", attention)
                QK = ka.sb("QK", [P, 2 * B_WIDTH // P, T])
                VS = ka.sb("VS", [P, 24, B_OUT])
                phase_qkv(nc, d["w_in"], c, hT, QK, VS, d["y"][N_EXPERTS * SLOTS:, :], d["ya"], yA)
                phase_attend(nc, c, d["attn"], QK, VS, ident, yB)
            yC = k.sb("yC", [P, C_WIDTH // P, T])
            phase_gmlp(nc, d["z_channel"][3 * D:, :], d["z_token"], d["sgu_ws"], d["sgu_bs"], d["sgu_ln_w"], d["sgu_ln_b"], c, hT, ident, yC)
            mT = k.sb("mT", [P, KT, T])
            phase_merge(nc, d["z_channel"], d["w_pa"], d["w_pb"], d["w_pc"], yA, yB, yC, table, mT)
            phase_out(nc, d["x"], d["w_out"], d["router_grp"], d["router_exp"], d["router_grp_b"], d["router_exp_b"],
                      mT, table, ident, d["x2"], d["h2"], LG)
        phase_route(nc, c, LG, ident, slot_u, wts, extra_i, d["tok"], tok_u)
        phase_experts(nc, d["moe_w1"], d["moe_w3"], d["moe_w2"], d["h2"], d["y"], table, ident, tok_u, extra_i)
        phase_final(nc, d["x2"], d["y"], d["norm_final"], slot_u, wts, out)


def kernel(**inputs):
    import concourse.bacc as bacc
    from concourse.bass_utils import run_bass_kernel_spmd as run

    nc = bacc.Bacc("TRN2", target_bir_lowering=False, num_devices=1)
    arrays, d, c = {}, {}, {}

    def give(name, a):
        a = np.ascontiguousarray(a)
        arrays[name] = a
        return nc.dram_tensor(name, a.shape, mybir.dt.from_np(a.dtype), kind="ExternalInput").ap()

    for name in ROWS:
        d[name] = give(name, inputs[name].reshape(-1, P))
    d["x"] = give("x", inputs["x"].reshape(T, D))
    for name in ("w_in", "w_decay2", "a2", "g2", "sgu_ws", "w_pa", "w_pb", "w_pc", "w_out", "router_grp", "router_exp",
                 "moe_w1", "moe_w3", "moe_w2"):
        d[name] = give(name, inputs[name][0])
    for name in ("sgu_bs", "sgu_ln_w", "sgu_ln_b", "router_grp_b", "router_exp_b", "norm_final"):
        d[name] = give(name, inputs[name].reshape(-1))
    for name, a in constants().items():
        c[name] = give("c_" + name, a)
    slots = (N_EXPERTS + MAX_EXTRA) * SLOTS
    for name, shape in (("attn", (3, T, OUT_W)), ("x2", (T, D)), ("h2", (T, D)),
                        ("ya", (D, T)), ("z_channel", (4 * D, T)), ("z_token", (T, C_WIDTH)), ("tok", (slots, 1)), ("y", (slots, D))):
        d[name] = nc.dram_tensor("s_" + name, shape, F32, kind="Internal").ap()
    out = nc.dram_tensor("out", (T, D), F32, kind="ExternalOutput").ap()
    program(nc, d, c, out)
    got = run(nc, [arrays], core_ids=[0]).results[0]["out"]
    return got.reshape(inputs["x"].shape)
```
